# Optimizing a Trainium2 kernel written in Bass

```python
import math
import jax, jax.numpy as jnp
from jax import lax
import numpy as np

D_MODEL = 1024
BATCH = 1
SEQ = 512
DEPTH = 2
DEC_BATCH = 8
DEC_SEQ = 4
PAST_LEN = 2048
PAGE_SIZE = 128

N_EVEN = (DEPTH + 1) // 2
N_ODD = DEPTH // 2
CONV_K = 3
EPS = 1e-6
A_WIDTH = D_MODEL // 2
B_HEADS = 8
B_KV_HEADS = 2
B_GROUP = B_HEADS // B_KV_HEADS
B_HEAD_DIM = (D_MODEL // 2) // B_HEADS
WINDOW = 128
AB_SPLITS = [A_WIDTH, 2 * A_WIDTH, 3 * A_WIDTH, 3 * A_WIDTH + B_HEADS * B_HEAD_DIM,
             3 * A_WIDTH + (B_HEADS + B_KV_HEADS) * B_HEAD_DIM]
D_IN_AB = 3 * A_WIDTH + (B_HEADS + 2 * B_KV_HEADS) * B_HEAD_DIM
D_MIX_AB = A_WIDTH + B_HEADS * B_HEAD_DIM
C_HEADS = 8
C_DK = 128
C_DV = D_MODEL // C_HEADS
C_DK_T = C_HEADS * C_DK
C_DV_T = C_HEADS * C_DV
D_IN_C = 2 * C_DK_T + 2 * C_DV_T
HGRN_CHUNK = 64
D_FF = ((8 * D_MODEL // 3 + 255) // 256) * 256

kernel_name = 'hybrid_shortconv_swa_hgrn2_convffn_step'

def rms_norm(x, g):
    x32 = x.astype(jnp.float32)
    y = x32 * lax.rsqrt(jnp.mean(x32 * x32, axis=-1, keepdims=True) + EPS) * g.astype(jnp.float32)
    return y.astype(x.dtype)

def causal_dwconv(u, prev, w):
    L = u.shape[1]
    full = jnp.concatenate([prev.astype(u.dtype), u], axis=1)
    y = full[:, 0:L] * w[0]
    for j in range(1, CONV_K):
        y = y + full[:, j:j + L] * w[j]
    return y, full[:, L:]

def alibi_slopes(n):
    return jnp.exp2(-8.0 * jnp.arange(1, n + 1, dtype=jnp.float32) / n)

def window_attention(qb, kb, vb, qpos, kpos, sinks):
    f32 = jnp.float32
    s = jnp.einsum('bnqkgd,bnskd->bnkgqs', qb.astype(f32), kb.astype(f32)) * (B_HEAD_DIM ** -0.5)
    dist = qpos[:, :, None] - kpos[:, None, :]
    valid = (kpos[:, None, :] >= 0) & (dist >= 0) & (dist < WINDOW)
    slopes = alibi_slopes(B_HEADS).reshape(B_KV_HEADS, B_GROUP)
    s = s - slopes[None, None, :, :, None, None] * dist.astype(f32)[None, :, None, None]
    s = jnp.where(valid[None, :, None, None], s, -jnp.inf)
    sink = sinks.astype(f32).reshape(1, 1, B_KV_HEADS, B_GROUP, 1)
    m = jnp.maximum(jnp.max(s, axis=-1), sink)
    p = jnp.exp(s - m[..., None])
    denom = jnp.sum(p, axis=-1) + jnp.exp(sink - m)
    o = jnp.einsum('bnkgqs,bnskd->bnqkgd', p / denom[..., None], vb.astype(f32))
    return o

def mixer_ab(xn, conv_prev, k_buf, v_buf, w_in, conv_w, sinks, w_out):
    Bsz, L, _ = xn.shape
    h, gb, gc, q, k, v = jnp.split(xn @ w_in, AB_SPLITS, axis=-1)
    ya, new_conv = causal_dwconv(gc * h, conv_prev, conv_w)
    ya = gb * ya
    q = q.reshape(Bsz, L, B_KV_HEADS, B_GROUP, B_HEAD_DIM)
    k = k.reshape(Bsz, L, B_KV_HEADS, B_HEAD_DIM)
    v = v.reshape(Bsz, L, B_KV_HEADS, B_HEAD_DIM)
    if k_buf is None:
        nb = L // WINDOW
        qb = q.reshape(Bsz, nb, WINDOW, B_KV_HEADS, B_GROUP, B_HEAD_DIM)
        pad = jnp.zeros((Bsz, WINDOW, B_KV_HEADS, B_HEAD_DIM), k.dtype)
        kp = jnp.concatenate([pad, k], axis=1).reshape(Bsz, nb + 1, WINDOW, B_KV_HEADS, B_HEAD_DIM)
        vp = jnp.concatenate([pad, v], axis=1).reshape(Bsz, nb + 1, WINDOW, B_KV_HEADS, B_HEAD_DIM)
        kb = jnp.concatenate([kp[:, :-1], kp[:, 1:]], axis=2)
        vb = jnp.concatenate([vp[:, :-1], vp[:, 1:]], axis=2)
        start = jnp.arange(nb, dtype=jnp.int32)[:, None] * WINDOW
        qpos = start + jnp.arange(WINDOW, dtype=jnp.int32)[None]
        kpos = start - WINDOW + jnp.arange(2 * WINDOW, dtype=jnp.int32)[None]
        keep = min(WINDOW, L)
        new_k, new_v = k[:, L - keep:], v[:, L - keep:]
    else:
        Wb = k_buf.shape[1]
        kc = jnp.concatenate([k_buf.astype(k.dtype), k], axis=1)
        vc = jnp.concatenate([v_buf.astype(v.dtype), v], axis=1)
        qb, kb, vb = q[:, None], kc[:, None], vc[:, None]
        qpos = (PAST_LEN + jnp.arange(L, dtype=jnp.int32))[None]
        kpos = (PAST_LEN - Wb + jnp.arange(Wb + L, dtype=jnp.int32))[None]
        new_k, new_v = kc[:, L:], vc[:, L:]
    yb = window_attention(qb, kb, vb, qpos, kpos, sinks).reshape(Bsz, L, B_HEADS * B_HEAD_DIM).astype(xn.dtype)
    out = jnp.concatenate([ya, yb], axis=-1) @ w_out
    return out, new_conv, new_k, new_v

def gla_chunked(q, k, v, log_f, S0):
    Bsz, L, H, DK = q.shape
    DV = v.shape[-1]
    C = math.gcd(HGRN_CHUNK, L)
    n = L // C
    def to_chunks(a):
        return a.reshape(Bsz, n, C, H, a.shape[-1]).transpose(1, 0, 3, 2, 4)
    causal = jnp.tril(jnp.ones((C, C), dtype=bool))
    def step(S, inp):
        qc, kc, vc, lc = inp
        G = jnp.cumsum(lc, axis=2)
        diff = G[:, :, :, None, :] - G[:, :, None, :, :]
        decay = jnp.exp(jnp.where(causal[:, :, None], diff, -jnp.inf))
        A = jnp.einsum('bhtd,bhsd,bhtsd->bhts', qc, kc, decay)
        o = jnp.einsum('bhts,bhse->bhte', A, vc) + jnp.einsum('bhtd,bhde->bhte', qc * jnp.exp(G), S)
        Gl = G[:, :, -1]
        S = jnp.exp(Gl)[..., None] * S + jnp.einsum('bhsd,bhse->bhde', kc * jnp.exp(Gl[:, :, None] - G), vc)
        return S, o
    S, o = lax.scan(step, S0, (to_chunks(q), to_chunks(k), to_chunks(v), to_chunks(log_f)))
    o = o.transpose(1, 0, 3, 2, 4).reshape(Bsz, L, H, DV)
    return o, S

def hgrn_lower_bounds(logits):
    pr = jax.nn.softmax(logits.astype(jnp.float32), axis=0)
    return jnp.clip(jnp.cumsum(pr, axis=0) - pr[0:1], 0.0, 1.0)

def mixer_c(xn, S0, w_in, lb, norm_g, w_out):
    Bsz, L, _ = xn.shape
    f32 = jnp.float32
    q, f, i, g = jnp.split(xn @ w_in, [C_DK_T, 2 * C_DK_T, 2 * C_DK_T + C_DV_T], axis=-1)
    fl = f.astype(f32)
    log_f = jnp.logaddexp(jnp.log(lb), jnp.log1p(-lb) + jax.nn.log_sigmoid(fl))
    k_in = (1.0 - lb) * jax.nn.sigmoid(-fl)
    shp = (Bsz, L, C_HEADS, C_DK)
    o, S = gla_chunked(q.astype(f32).reshape(shp), k_in.reshape(shp),
                       i.astype(f32).reshape(Bsz, L, C_HEADS, C_DV), log_f.reshape(shp), S0.astype(f32))
    o = rms_norm(o, norm_g).reshape(Bsz, L, C_DV_T) * jax.nn.silu(g.astype(f32))
    return o.astype(xn.dtype) @ w_out, S.astype(S0.dtype)

def conv_ffn(xn, prev, w_up, conv_w, w_down):
    a, b = jnp.split(xn @ w_up, 2, axis=-1)
    a, new_prev = causal_dwconv(a, prev, conv_w)
    return (jax.nn.gelu(a) * b) @ w_down, new_prev

def run_trunk(x, conv_a_prev, k_buf, v_buf, hgrn_prev, ffn_prev, p):
    conv_new, k_new, v_new, s_new, ffn_new = [], [], [], [], []
    lbs = hgrn_lower_bounds(p['hgrn_lb_logits'])
    for l in range(DEPTH):
        j = l // 2
        h = rms_norm(x, p['norm_mix_pre'][l])
        if l % 2 == 0:
            mix, c, kk, vv = mixer_ab(h, conv_a_prev[j], None if k_buf is None else k_buf[j],
                                      None if v_buf is None else v_buf[j], p['w_in_ab'][j],
                                      p['conv_a_w'][j], p['attn_sinks'][j], p['w_out_ab'][j])
            conv_new.append(c); k_new.append(kk); v_new.append(vv)
        else:
            mix, S = mixer_c(h, hgrn_prev[j], p['w_in_c'][j], lbs[l], p['hgrn_norm_g'][j], p['w_out_c'][j])
            s_new.append(S)
        x = x + rms_norm(mix, p['norm_mix_post'][l])
        h = rms_norm(x, p['norm_ffn_pre'][l])
        fo, fs = conv_ffn(h, ffn_prev[l], p['w_ffn_up'][l], p['ffn_conv_w'][l], p['w_ffn_down'][l])
        ffn_new.append(fs)
        x = x + rms_norm(fo, p['norm_ffn_post'][l])
    return x, jnp.stack(conv_new), jnp.stack(k_new), jnp.stack(v_new), jnp.stack(s_new), jnp.stack(ffn_new)

def setup_inputs(seed: int = 0) -> dict:
    key = jax.random.key(seed)
    ks = jax.random.split(key, 24)
    f32 = jnp.float32
    def nrm(k, shape, scale=1.0):
        return scale * jax.random.normal(k, shape, f32)
    win_buf = min(WINDOW, PAST_LEN)
    return {
        'x_prompt': nrm(ks[0], (BATCH, SEQ, D_MODEL)),
        'x_sample': nrm(ks[1], (DEC_BATCH, DEC_SEQ, D_MODEL)),
        'state_conv_a': nrm(ks[2], (N_EVEN, DEC_BATCH, CONV_K - 1, A_WIDTH)),
        'cache_swa_k': nrm(ks[3], (N_EVEN, DEC_BATCH, win_buf, B_KV_HEADS, B_HEAD_DIM)),
        'cache_swa_v': nrm(ks[4], (N_EVEN, DEC_BATCH, win_buf, B_KV_HEADS, B_HEAD_DIM)),
        'state_hgrn': nrm(ks[5], (N_ODD, DEC_BATCH, C_HEADS, C_DK, C_DV), 0.3),
        'state_ffn_conv': nrm(ks[6], (DEPTH, DEC_BATCH, CONV_K - 1, D_FF), 0.5),
        'norm_mix_pre': 1.0 + nrm(ks[7], (DEPTH, D_MODEL), 0.02),
        'norm_mix_post': 1.0 + nrm(ks[8], (DEPTH, D_MODEL), 0.02),
        'norm_ffn_pre': 1.0 + nrm(ks[9], (DEPTH, D_MODEL), 0.02),
        'norm_ffn_post': 1.0 + nrm(ks[10], (DEPTH, D_MODEL), 0.02),
        'w_in_ab': nrm(ks[11], (N_EVEN, D_MODEL, D_IN_AB), D_MODEL ** -0.5),
        'conv_a_w': nrm(ks[12], (N_EVEN, CONV_K, A_WIDTH), CONV_K ** -0.5),
        'attn_sinks': nrm(ks[13], (N_EVEN, B_HEADS)),
        'w_out_ab': nrm(ks[14], (N_EVEN, D_MIX_AB, D_MODEL), D_MIX_AB ** -0.5),
        'w_in_c': nrm(ks[15], (N_ODD, D_MODEL, D_IN_C), D_MODEL ** -0.5),
        'hgrn_lb_logits': nrm(ks[16], (DEPTH, C_DK_T)),
        'hgrn_norm_g': 1.0 + nrm(ks[17], (N_ODD, C_DV), 0.02),
        'w_out_c': nrm(ks[18], (N_ODD, C_DV_T, D_MODEL), C_DV_T ** -0.5),
        'w_ffn_up': nrm(ks[19], (DEPTH, D_MODEL, 2 * D_FF), D_MODEL ** -0.5),
        'ffn_conv_w': nrm(ks[20], (DEPTH, CONV_K, D_FF), CONV_K ** -0.5),
        'w_ffn_down': nrm(ks[21], (DEPTH, D_FF, D_MODEL), D_FF ** -0.5),
    }

def reference(x_prompt, x_sample, state_conv_a, cache_swa_k, cache_swa_v, state_hgrn, state_ffn_conv,
              norm_mix_pre, norm_mix_post, norm_ffn_pre, norm_ffn_post, w_in_ab, conv_a_w, attn_sinks,
              w_out_ab, w_in_c, hgrn_lb_logits, hgrn_norm_g, w_out_c, w_ffn_up, ffn_conv_w, w_ffn_down):
    p = dict(norm_mix_pre=norm_mix_pre, norm_mix_post=norm_mix_post, norm_ffn_pre=norm_ffn_pre,
             norm_ffn_post=norm_ffn_post, w_in_ab=w_in_ab, conv_a_w=conv_a_w, attn_sinks=attn_sinks,
             w_out_ab=w_out_ab, w_in_c=w_in_c, hgrn_lb_logits=hgrn_lb_logits, hgrn_norm_g=hgrn_norm_g,
             w_out_c=w_out_c, w_ffn_up=w_ffn_up, ffn_conv_w=ffn_conv_w, w_ffn_down=w_ffn_down)
    Bp = x_prompt.shape[0]
    dt = x_prompt.dtype
    y_prompt, conv_p, k_p, v_p, hgrn_p, ffn_p = run_trunk(
        x_prompt,
        jnp.zeros((N_EVEN, Bp, CONV_K - 1, A_WIDTH), dt), None, None,
        jnp.zeros((N_ODD, Bp, C_HEADS, C_DK, C_DV), dt),
        jnp.zeros((DEPTH, Bp, CONV_K - 1, D_FF), dt), p)
    y_sample, conv_s, k_s, v_s, hgrn_s, ffn_s = run_trunk(
        x_sample, state_conv_a, cache_swa_k, cache_swa_v, state_hgrn, state_ffn_conv, p)
    return (y_prompt, y_sample, conv_p, conv_s, k_p, k_s, v_p, v_s, hgrn_p, hgrn_s, ffn_p, ffn_s)


_drawn_inputs = setup_inputs


def setup_inputs(seed=0):
    import zlib

    import numpy as np

    out = dict(_drawn_inputs(seed))
    spreads = {}
    factors = {'norm_ffn_post': 2.914, 'hgrn_norm_g': 5.283}
    for name, (base, spread) in spreads.items():
        noise = np.random.default_rng([zlib.crc32(name.encode()), seed]).standard_normal(out[name].shape)
        drawn = base * np.exp(spread * noise) if base else spread * noise
        out[name] = __import__('jax').numpy.asarray(drawn.astype(out[name].dtype))
    for name, factor in factors.items():
        out[name] = (out[name] * factor).astype(out[name].dtype)
    return out
```

```python
from contextlib import ExitStack

import numpy as np

import concourse.bass as bass
from concourse import mybir

F32 = mybir.dt.float32
F32R = mybir.dt.float32r
I32 = mybir.dt.int32
ALU = mybir.AluOpType
ACT = mybir.ActivationFunctionType
AX_X = mybir.AxisListType.X

P = 128
D = 1024
TP, NB, TS = 512, 8, 4
T = TP + NB * TS
H = T // 2
KD = D // P
A_W = 512
CA = A_W // P
WIN = 128
NBLK = TP // WIN
HD = 64
GRP = 4
DFF = 2816
KF = DFF // P
KFH = KF // 2
HEADS = 8
CH = 128
NCH = TP // CH
SPANS = (64, 32, 16, 8)
EPS = 1e-6
F_FLOOR = 2e-9
NEG = -1e30

PHASES = [("in_ab", 18, 8), ("out_ab", 8, 8), ("up0", 2 * KF, 8), ("down0", 2 * KD, KFH),
          ("in_c", 4 * HEADS, 8), ("out_c", 8, 8), ("up1", 2 * KF, 8), ("down1", 2 * KD, KFH)]
UNIT0, TILE0, _n, _t = {}, {}, 0, 0
for _name, _units, _kt in PHASES:
    UNIT0[_name], TILE0[_name] = _n, _t
    _n += _units
    _t += _units if _kt == 8 else _units // 2
UNITS = _n

V_GAIN = 0
V_CONVA = V_GAIN + 64
V_CONVF = V_CONVA + 3 * CA
V_LB = V_CONVF + 2 * 3 * KF
V_NG = V_LB + 16
V_SINK = V_NG + 1
V_SINKS = V_SINK + 8
NV = V_SINKS + 1
MIX_PRE, MIX_POST, FFN_PRE, FFN_POST = range(4)


def gain_col(kind, layer):
    return V_GAIN + (kind * 2 + layer) * KD


def half_of(m):
    n, h = divmod(m, 2)
    kt = [k for name, u, k in PHASES if UNIT0[name] <= n < UNIT0[name] + u][0]
    first = (kt + 1) // 2
    return n, h, (0, first)[h], (first, kt - first)[h]


HALF = (KFH + 1) // 2 * P


class Steps:

    def __init__(self, sem):
        self.sem, self.n = sem, 0

    def mark(self, ins):
        ins.then_inc(self.sem, 1)
        self.n = self.n + 1

    def wait(self, eng):
        eng.wait_ge(self.sem, self.n)


def shape_tables():
    slopes = np.exp2(-8.0 * np.arange(1, 9, dtype=np.float32) / 8)
    q, k = np.arange(P)[:, None], np.arange(2 * WIN)[None]
    dist = q + WIN - k
    ok = (dist >= 0) & (dist < WIN)
    bias = np.where(ok[:, None], -slopes[None, :, None] * dist[:, None], NEG).astype(np.float32)
    row = np.arange(P)
    g, j, t = row // 16 % 2, row // 4 % 4, row % 4
    dist = t[:, None] + WIN - np.arange(WIN + TS)[None]
    ok = (dist >= 0) & (dist < WIN)
    bias_s = np.where(ok, -slopes[4 * g + j][:, None] * dist, NEG).astype(np.float32)
    s, t = np.arange(CH)[:, None], np.arange(CH)[None]
    masks = [(s // 8 == t // 8) & (s <= t)]
    for h in SPANS:
        masks.append((s // (2 * h) == t // (2 * h)) & (s % (2 * h) < h) & (t % (2 * h) >= h))
    masks = np.stack(masks, 1).astype(np.int32)
    s, t = np.arange(NB * TS)[:, None], np.arange(NB * TS)[None]
    mask_s = ((s // TS == t // TS) & (s <= t)).astype(np.int32)
    own = (np.arange(NB * TS)[:, None] // TS == np.arange(NB)[None]).astype(np.float32)
    own = np.repeat(own[:, :, None], P, 2)
    keep = np.ones((P, T), np.float32)
    keep[:, 0:TP:CH] = 0
    keep[:, TP::TS] = 0
    return {"c_ident": np.eye(P, dtype=np.float32), "c_bias": bias, "c_bias_s": bias_s,
            "c_masks": masks, "c_mask_s": mask_s, "c_own": own, "c_keep": keep}


def build(nc, dram):
    ctx = ExitStack()

    def sb(name, shape, dt=F32, at=ctx):
        return at.enter_context(nc.sbuf_tensor(name, shape, dt))

    def bank(name):
        return ctx.enter_context(nc.psum_tensor(name, [P, 512], F32))

    def sem(name):
        return ctx.enter_context(nc.semaphore(name))

    with ctx:
        x = sb("x", [P, KD, T])
        rstd = sb("rstd", [P, T])
        S = [sb(f"scratch{i}", [P, T]) for i in range(4)]
        vec = sb("vec", [P, NV])
        lb = sb("lb", [P, 8, HEADS])
        eps = sb("eps", [P, 1])
        arrival = sb("arrival", [P, 6])
        ones = sb("ones", [P, P])
        ident = sb("ident", [P, P])
        sp = sb("sp", [P, NB, 2 + TS])
        st_f = sb("st_f", [P, 2, KF, NB, 2])
        tail_f = sb("tail_f", [P, 2, KF, 2])
        st_a = sb("st_a", [P, CA, NB, 2])
        tail_a = sb("tail_a", [P, CA, 2])
        raw = [sb(f"raw{i}", [P, KFH * P]) for i in range(4)]
        w_hi = [sb(f"w_hi{i}", [P, KFH * P], F32R) for i in range(2)]
        w_lo = [sb(f"w_lo{i}", [P, KFH * P], F32R) for i in range(2)]

        with ExitStack() as at:
            h_hi = sb("h_hi", [P, KD, T], F32R, at)
            h_lo = sb("h_lo", [P, KD, T], F32R, at)
        with ExitStack() as at:
            mix = sb("mix", [P, KD, T], F32, at)
            over = sb("mix_rest", [P, KD, T], F32, at)
            with ExitStack() as a:
                y_hi = sb("y_hi", [P, KD, T], F32R, a)
                y_lo = sb("y_lo", [P, KD, T], F32R, a)
                with ExitStack() as b:
                    q_sb = sb("q_sb", [P, GRP, T], F32, b)
                    k_sb = sb("k_sb", [P, T], F32, b)
                    v_sb = sb("v_sb", [P, T], F32, b)
                    kc = sb("kc", [P, NB, WIN + TS], F32, b)
                    vc = sb("vc", [P, NB, P], F32, b)
                    vnew = sb("vnew", [TS, NB, P], F32, b)
                    vtok = sb("vtok", [P, NBLK, P], F32, b)
                    qbd = sb("qbd", [P, NB, 2 * GRP * TS], F32, b)
                    bias = sb("bias", [P, 8, 2 * WIN], F32, b)
                    bias_s = sb("bias_s", [P, WIN + TS], F32, b)
                    pr = [sb(f"pr{i}", [P, GRP, 2 * WIN], F32, b) for i in range(2)]
                    pr_s = sb("pr_s", [P, 2, WIN + TS], F32, b)
                    pT = sb("pT", [P, 2, GRP * P], F32, b)
                    pT_s = sb("pT_s", [P, 2, P], F32, b)
                    pT_n = sb("pT_n", [TS, 2, P], F32, b)
                    sm = sb("sm", [P, 2, 6, GRP], F32, b)
                    sm_s = sb("sm_s", [P, 6, 2], F32, b)
                with ExitStack() as b:
                    kk, G, qn, vv, gn, sg, eG, kd, qG, E1, E2 = [
                        sb(f"c_{n}", [P, T], F32, b)
                        for n in ("kk", "G", "qn", "vv", "gn", "sg", "eG", "kd", "qG", "E1", "E2")]
                    lev = [sb(f"lev{i}", [P, TP], F32, b) for i in range(len(SPANS))]
                    AT = sb("AT", [P, TP], F32, b)
                    AT_s = sb("AT_s", [NB * TS, NB * TS], F32, b)
                    Sst = sb("Sst", [P, NCH, P], F32, b)
                    vt = sb("vt", [P, NCH, P], F32, b)
                    vt_s = sb("vt_s", [NB * TS, P], F32, b)
                    kt = sb("kt", [P, NCH, P], F32, b)
                    kt_s = sb("kt_s", [NB * TS, P], F32, b)
                    S0 = sb("S0", [P, NB, P], F32, b)
                    Snew = sb("Snew", [P, NB, P], F32, b)
                    vbd = sb("vbd", [NB * TS, NB, P], F32, b)
                    own = sb("own", [NB * TS, NB, P], F32, b)
                    masks = sb("masks", [P, 1 + len(SPANS), CH], I32, b)
                    mask_s = sb("mask_s", [NB * TS, NB * TS], I32, b)
                    keep = sb("keep", [P, T], F32, b)
            with ExitStack() as a:
                g_hi = sb("g_hi", [P, KF, T], F32R, a)
                g_lo = sb("g_lo", [P, KF, T], F32R, a)

        acc = [ctx.enter_context(nc.psum_tensor(f"acc{i}", [P, 2, 512], F32)) for i in range(2)]
        A = [bank(f"aux{i}") for i in range(4)]

        raw_ready = [sem(f"raw_ready{i}") for i in range(4)]
        hi_ready = sem("hi_ready")
        lo_ready = sem("lo_ready")
        half_done = sem("half_done")
        evac = sem("evac")
        x_in = [sem(f"x_in{k}") for k in range(KD)]
        const_in = sem("const_in")
        const_a = sem("const_a")
        const_c = sem("const_c")
        state0_in = sem("state0_in")
        stored = sem("stored")
        stored_late = sem("stored_late")
        x_out = sem("x_out")
        state_out = sem("state_out")
        set_up = sem("set_up")
        h_hi_ready = sem("h_hi_ready")
        h_ready = sem("h_ready")
        x_new = sem("x_new")
        sq_ready = sem("sq_ready")
        sq_added = sem("sq_added")
        mix_scaled = sem("mix_scaled")
        stat_done = sem("stat_done")
        rstd_ready = sem("rstd_ready")
        sp_ready = sem("sp_ready")
        tap_ready = sem("tap_ready")
        conv_done = sem("conv_done")
        act_done = sem("act_done")
        gate_ready = sem("gate_ready")
        g_hi_ready = sem("g_hi_ready")
        g_ready = sem("g_ready")
        act_step, dve_step, pool_step = sem("act_step"), sem("dve_step"), sem("pool_step")
        qbd_ready, kc_ready = sem("qbd_ready"), sem("kc_ready")
        vT_done, vT_copied = sem("vT_done"), sem("vT_copied")
        s_done, s_biased, p_exp, p_sum, p_ready = [sem(n) for n in
                                                   ("s_done", "s_biased", "p_exp", "p_sum", "p_ready")]
        pT_done, pT_copied, o_done, yb_hi, yb_lo = [sem(n) for n in
                                                    ("pT_done", "pT_copied", "o_done", "yb_hi", "yb_lo")]
        names = ("fl_ready", "sig_ready", "ff_ready", "lf_ready", "G_ready", "eG_ready", "qG_ready",
                 "kd_diff", "kd_exp", "kd_ready", "lev_diff", "lev_exp", "lev_ready", "diag_diff", "diag_exp",
                 "diag_ready", "al_done", "al_taken", "u_done", "us_done", "st_ready", "oc_done",
                 "osq_ready", "ostat_done", "ors_ready", "og_ready", "oy_ready", "oy_hi", "oy_lo",
                 "kdT_done", "kdT_copied", "vcT_done", "vcT_copied", "vbd_ready", "gn_ready",
                 "sg_ready", "gs_ready", "s0_scaled", "snew_ready", "lb_ready", "lb_done")
        C = {n: sem(n) for n in names}

        def tile(name, i):
            return TILE0[name] + i + 1

        def tok2(ap):
            return ap.rearrange("p (a b) -> p a b", a=2)

        def sample(ap, n=TS):
            return ap.rearrange("p (b t) -> p b t", b=NB)

        def later(ap, span):
            return ap.rearrange("p (n a s) -> p n a s", a=2, s=span)[:, :, 1, :]

        acc_v = [a[:, :, 0:H] for a in acc]
        block = ctx.enter_context(nc.Block())

        @block.sync
        def _(sp_q):
            for k in range(KD):
                sp_q.dma_start(x[:, k, :], dram["xT"][:, k, :]).then_inc(x_in[k], 16)
                if k == 0:
                    sp_q.dma_start(vec[:], dram["vec"]).then_inc(const_in, 16)
                    sp_q.dma_start(ident[:], dram["c_ident"]).then_inc(const_in, 16)
                    sp_q.dma_start(st_a[:], dram["st_a"]).then_inc(const_in, 16)
                    sp_q.dma_start(st_f[:], dram["st_f"]).then_inc(const_in, 16)

            def unit(name, u, i):
                n, kt_ = UNIT0[name] + u, half_of(2 * UNIT0[name])[3] + half_of(2 * UNIT0[name] + 1)[3]
                if not isinstance(i, int) or n + 4 * i >= 4:
                    sp_q.wait_ge(lo_ready, 2 * (n + 4 * i) - 6)
                src = dram["w_" + name]
                sp_q.dma_start(raw[n % 4][:, 0:kt_ * P], src[u + 4 * i, :, :]
                               ).then_inc(raw_ready[n % 4], 16)

            for name, units, kt_ in PHASES:
                if name == "in_ab":
                    for u in range(units):
                        unit(name, u, 0)
                        if u == 3:
                            sp_q.dma_start(kc[:, :, 0:WIN], dram["kcT"]).then_inc(const_a, 16)
                            sp_q.dma_start(vc[:], dram["vc"].rearrange("b k f -> k b f")).then_inc(const_a, 16)
                            sp_q.dma_start(bias[:], dram["c_bias"]).then_inc(const_a, 16)
                            sp_q.dma_start(bias_s[:], dram["c_bias_s"]).then_inc(const_a, 16)
                    continue
                with sp_q.Fori(0, units // 4) as i:
                    for u in range(4):
                        unit(name, u, i)
            for k in range(KD):
                sp_q.wait_ge(x_new, 3 * KD + k + 1)
                sp_q.dma_start(dram["o_x"][:, k, :], x[:, k, :]).then_inc(x_out, 16)
            sp_q.wait_ge(x_out, 16 * KD)

        @block.tensor
        def _(pe):
            def half(m, off, out, moving, kt_base, start, stop, tile_waits=None, ks=None, signal=1):
                n, half_, _, kts = half_of(m + off if isinstance(off, int) else m)
                slot = n % 2
                pe.wait_ge(lo_ready, m + 1 + off)
                for k in ks or range(kts):
                    cols = slice(half_ * HALF + k * P, half_ * HALF + (k + 1) * P)
                    kk_ = kt_base + k
                    if tile_waits is not None:
                        pe.wait_ge(*tile_waits(kk_))
                    passes = [(w_hi, moving[0]), (w_hi, moving[1]), (w_lo, moving[0])]
                    for q, (w, mv) in enumerate(passes):
                        for t in range(2):
                            mm = pe.matmul(acc[out][:, t, 0:H], w[slot][:, cols], mv[:, kk_, t * H:(t + 1) * H],
                                           start=start and k == 0 and q == 0, stop=stop and k == kts - 1 and q == 2)
                if signal:
                    mm.then_inc(half_done, signal)

            def stats(norm):
                for src, ready, count in ((S[2], sq_added, KD - 1), (S[1], sq_ready, KD)):
                    pe.wait_ge(ready, count * (norm + 1))
                    for t in range(2):
                        mm = pe.matmul(A[t][:, 0:H], ones[:], src[:, t * H:(t + 1) * H], start=src is S[2],
                                       stop=src is S[1])
                        if src is S[1]:
                            mm.then_inc(stat_done, 1)

            def tile_ready(norm):
                return lambda k: (h_ready, KD * norm + k + 1)

            h = (h_hi, h_lo)
            def values_transposed(part):
                if part == 0:
                    pe.wait_ge(evac, tile("in_ab", 5))
                    for n in range(NBLK):
                        mm = pe.transpose(A[2][:, n * P:(n + 1) * P], v_sb[:, n * P:(n + 1) * P], ident[:])
                else:
                    b0 = 4 * (part - 1)
                    if part == 2:
                        pe.wait_ge(vT_copied, 1)
                    for b in range(4):
                        c = TP + (b0 + b) * TS
                        mm = pe.transpose(A[4 - part][0:TS, b * P:(b + 1) * P], v_sb[:, c:c + TS], ident[:])
                mm.then_inc(vT_done, 1)

            def sample_scores():
                pe.wait_ge(qbd_ready, 2)
                pe.wait_ge(kc_ready, 1)
                pe.wait_ge(const_a, 64)
                for b in range(NB):
                    r = 32 * (b % 4)
                    mm = pe.matmul(A[b // 4][r:r + 32, 0:WIN + TS], qbd[:, b, :], kc[:, b, :], start=True, stop=True)
                mm.then_inc(s_done, 1)

            def sample_probs_transposed():
                pe.wait_ge(p_ready, 1)
                pe.wait_ge(vT_copied, 3)
                for c in range(2):
                    pe.transpose(A[2][:, c * P:(c + 1) * P], pr_s[:, c, 0:WIN], ident[:])
                    mm = pe.transpose(A[3][0:TS, c * P:(c + 1) * P], pr_s[:, c, WIN:WIN + TS], ident[:])
                mm.then_inc(pT_done, 1)

            def sample_out():
                pe.wait_ge(pT_copied, 2)
                for b in range(NB):
                    r = 32 * (b % 4)
                    pe.matmul(A[2][:, 32 * b:32 * b + 32], vc[:, b, :], pT_s[:, b // 4, r:r + 32], start=True, stop=False)
                    mm = pe.matmul(A[2][:, 32 * b:32 * b + 32], vnew[:, b, :], pT_n[:, b // 4, r:r + 32],
                                   start=False, stop=True)
                mm.then_inc(o_done, 1)

            def scores(s):
                n, g = divmod(s, 2)
                lo_k = WIN if n == 0 else 0
                rows = slice(64 * g, 64 * g + 64)
                pe.wait_ge(s_biased, 2 * s + 2)
                for j in range(GRP):
                    mm = pe.matmul(A[j // 2][:, (j % 2) * 256 + lo_k:(j % 2) * 256 + 256],
                                   q_sb[rows, j, n * WIN:(n + 1) * WIN],
                                   k_sb[rows, (n - 1) * WIN + lo_k:(n + 1) * WIN], start=True, stop=True)
                mm.then_inc(s_done, 1)

            def probs_transposed(s):
                pe.wait_ge(p_ready, s + 2)
                pe.wait_ge(yb_lo, s + 1)
                if s:
                    pe.wait_ge(pT_copied, 2 * s + 2)
                for c in range(1 if s < 2 else 0, 2):
                    for j in range(GRP):
                        mm = pe.transpose(A[2 + c][:, j * P:(j + 1) * P], pr[s % 2][:, j, c * WIN:(c + 1) * WIN], ident[:])
                mm.then_inc(pT_done, 1)

            def attention_out(s):
                n, g = divmod(s, 2)
                pe.wait_ge(pT_copied, 2 * s + 4)
                first = 1 if n == 0 else 0
                for c in range(first, 2):
                    mm = pe.matmul(A[2][64 * g:64 * g + 64, :], vtok[:, n - 1 + c, 64 * g:64 * g + 64], pT[:, c, :],
                                   start=c == first, stop=c == 1)
                mm.then_inc(o_done, 1)

            extra = {11: [lambda: values_transposed(0), lambda: values_transposed(1)],
                     12: [lambda: values_transposed(2), sample_scores],
                     15: [sample_probs_transposed], 16: [sample_out]}
            for s in range(8):
                extra.setdefault(14 + 2 * s, []).append(lambda s=s: scores(s))
                extra.setdefault(17 + 2 * s, []).append(lambda s=s: probs_transposed(s))
                extra.setdefault(18 + 2 * s, []).append(lambda s=s: attention_out(s))
            pe.wait_ge(set_up, 3)
            pe.wait_ge(const_in, 64)
            for u in range(18):
                if u >= 2:
                    pe.wait_ge(evac, u - 1)
                for e in range(2):
                    m = 2 * u + e
                    half(m, 0, u % 2, h, 4 * e, e == 0, e == 1, tile_ready(0) if u == 0 else None)
                    if m == 2:
                        stats(0)
                    for f in extra.get(m, []):
                        f()

            def out_phase(name, moving, norm, ready, first=0):
                for tile in range(first, KD):
                    pe.wait_ge(evac, TILE0[name] + tile - 1)
                    for e in range(2):
                        m = 2 * (UNIT0[name] + tile) + e
                        half(m, 0, tile % 2, moving, 4 * e, e == 0, e == 1, ready if tile == 0 else None)
                stats(norm)

            def yb_ready(k):
                return (g_ready, k + 1) if k < CA else (yb_lo, 9)

            out_phase("out_ab", (y_hi, y_lo), 1, yb_ready)

            def ffn(layer):
                name = f"up{layer}"
                norm = 2 + 4 * layer

                def up(i, peeled_first):
                    for u in range(4):
                        pe.wait_ge(evac, TILE0[name] + u - 1 + 4 * i)
                        for e in range(2):
                            half(2 * (UNIT0[name] + u) + e, 8 * i, u % 2, h, 4 * e, e == 0, e == 1,
                                 tile_ready(norm // 2) if peeled_first and u == 0 else None)
                            if peeled_first and u == 1 and e == 0:
                                stats(norm)

                up(0, True)
                with pe.Fori(1, KF // 2) as i:
                    up(i, False)
                name = f"down{layer}"

                def down(i, peeled_first):
                    for tile in range(2):
                        pe.wait_ge(evac, TILE0[name] + tile - 1 + 2 * i)
                        for r in range(2):
                            if peeled_first and tile == 0:
                                pe.wait_ge(g_ready, CA + KF * layer + (KFH, KF)[r])
                            for e in range(2):
                                half(2 * (UNIT0[name] + 2 * tile + r) + e, 8 * i, tile, (g_hi, g_lo),
                                     KFH * r + 6 * e, r == 0 and e == 0, r == 1 and e == 1)

                down(0, True)
                with pe.Fori(1, KD // 2) as i:
                    down(i, False)
                stats(norm + 1)

            ffn(0)

            def levels(hd, which):
                b = (1, 2, 3, 0, 1)[which]
                lhs, rhs = (E2, E1) if which == 0 else (lev[which - 1], lev[which - 1])
                for c in range(NCH):
                    cs = slice(c * CH, (c + 1) * CH)
                    out, moving = A[b][:, cs], rhs[:, cs]
                    if which:
                        out = A[b][:, c * (CH // 2):(c + 1) * (CH // 2)]
                        moving = later(moving, SPANS[which - 1])
                    mm = pe.matmul(out, lhs[:, cs], moving, start=True, stop=True)
                mm.then_inc(C["al_done"], 1)

            def hgrn_tick(t, prev, cur):
                if prev is not None:
                    if t == 0:
                        pe.wait_ge(C["vbd_ready"], prev + 1)
                        pe.matmul(A[3][:, :], kt_s[:], vbd[:, 0:4, :], start=True, stop=True
                                  ).then_inc(C["us_done"], 1)
                        pe.wait_ge(C["diag_ready"], 2 * prev + 2)
                        pe.wait_ge(C["vcT_copied"], prev + 1)
                        pe.matmul(A[0][:, :], kt_s[:], vbd[:, 4:8, :], start=True, stop=True
                                  ).then_inc(C["us_done"], 1)
                        levels(prev, 0)
                        pe.wait_ge(C["st_ready"], prev + 1)
                        pe.matmul(A[2][0:NB * TS, 0:NB * TS], E2[:, TP:T], E1[:, TP:T], start=True, stop=True
                                  ).then_inc(C["al_done"], 1)
                    if t == 1:
                        pe.wait_ge(C["lev_ready"], 8 * prev + 8)
                        pe.wait_ge(C["al_taken"], 6 * prev + 2)
                        pe.wait_ge(C["snew_ready"], 2 * prev + 1)
                        levels(prev, 1)
                        levels(prev, 2)
                    if t == 2:
                        pe.wait_ge(C["snew_ready"], 2 * prev + 2)
                        levels(prev, 3)
                        levels(prev, 4)
                    if t == 3:
                        pe.wait_ge(C["al_taken"], 6 * prev + 6)
                        pe.wait_ge(C["qG_ready"], prev + 1)
                        pe.wait_ge(state0_in, 16 * prev + 16)
                        for c in range(NCH):
                            cs = slice(c * CH, (c + 1) * CH)
                            mm = pe.matmul(A[3][:, cs], vt[:, c, :], AT[:, cs], start=True, stop=c == 0)
                            if c:
                                mm = pe.matmul(A[3][:, cs], Sst[:, c - 1, :], qG[:, cs], start=False, stop=True)
                        pe.matmul(A[2][:, 0:NB * TS], vt_s[:], AT_s[:], start=True, stop=False,
                                  skip_group_check=True)
                        for b in range(NB):
                            mm = pe.matmul(A[2][:, b * TS:(b + 1) * TS], S0[:, b, :], qG[:, TP + b * TS:TP + (b + 1) * TS],
                                           start=False, stop=True, skip_group_check=True)
                        mm.then_inc(C["oc_done"], 1)
                    if t == 4:
                        pe.wait_ge(C["osq_ready"], prev + 1)
                        pe.matmul(A[0][:, 0:H], ones[:], S[2][:, 0:H], start=True, stop=True)
                        pe.matmul(A[1][:, 0:H], ones[:], S[2][:, H:T], start=True, stop=True
                                  ).then_inc(C["ostat_done"], 1)
                if cur is not None:
                    if t == 5:
                        pe.wait_ge(C["kd_ready"], cur + 1)
                        if prev is not None:
                            pe.wait_ge(C["ors_ready"], prev + 1)
                        for c in range(NCH):
                            pe.transpose(A[0][:, c * P:(c + 1) * P], kd[:, c * CH:(c + 1) * CH], ident[:])
                        pe.transpose(A[1][0:NB * TS, 0:P], kd[:, TP:T], ident[:]).then_inc(C["kdT_done"], 1)
                    if t == 6:
                        pe.wait_ge(evac, tile("in_c", 2) + 4 * cur)
                        pe.wait_ge(C["kdT_copied"], cur + 1)
                        for c in range(NCH):
                            pe.transpose(A[0][:, c * P:(c + 1) * P], vv[:, c * CH:(c + 1) * CH], ident[:])
                        pe.transpose(A[1][0:NB * TS, 0:P], vv[:, TP:T], ident[:]).then_inc(C["vcT_done"], 1)
                    if t == 7:
                        pe.wait_ge(C["vcT_copied"], cur + 1)
                        if prev is not None:
                            pe.wait_ge(C["og_ready"], prev + 1)
                        for c in range(NCH):
                            mm = pe.matmul(A[2][:, c * P:(c + 1) * P], kt[:, c, :], vt[:, c, :], start=True, stop=True)
                        mm.then_inc(C["u_done"], 1)

            def head(hd, prev, first):
                for u in range(4):
                    pe.wait_ge(evac, TILE0["in_c"] + u - 1 + 4 * hd)
                    for e in range(2):
                        half(2 * (UNIT0["in_c"] + u) + e, 8 * hd, u % 2, h, 4 * e, e == 0, e == 1,
                             tile_ready(2) if first and u == 0 else None)
                        if first and u == 1 and e == 0:
                            stats(4)
                        hgrn_tick(2 * u + e, prev, hd)

            head(0, None, True)
            with pe.Fori(1, HEADS) as hd:
                head(hd, hd - 1, False)

            def yc_ready(k):
                return (C["oy_lo"], k + 1)

            m = 2 * UNIT0["out_c"]
            for u in range(2):
                pe.wait_ge(evac, TILE0["out_c"] + u - 1)
                for e in range(2):
                    for t in ((0,), (1, 2), (3,), (4,))[2 * u + e]:
                        hgrn_tick(t, HEADS - 1, None)
                    half(m + 2 * u + e, 0, u, (y_hi, y_lo), 4 * e, e == 0, False, yc_ready if u == 0 else None,
                         ks=range(4 - e), signal=int(m + 2 * u + e == m))
            for u in range(2):
                half(m + 2 * u + 1, 0, u, (y_hi, y_lo), 4, False, True, yc_ready if u == 0 else None,
                     ks=[3], signal=1 + u)
            out_phase("out_c", (y_hi, y_lo), 5, None, first=2)
            ffn(1)

        @block.scalar
        def _(act):
            step = Steps(act_step)

            def split(m, off):
                s = m + off if isinstance(off, int) else m
                if s >= 2 * UNITS:
                    return
                n, h_, kt0, kts = half_of(s)
                if h_ == 0:
                    act.wait_ge(raw_ready[n % 4], 16 * ((m // 2) // 4 + 1) + (off * 2))
                if not isinstance(off, int) or s >= 4:
                    act.wait_ge(half_done, m - 3 + off)
                cols = slice(kt0 * P, (kt0 + kts) * P)
                act.copy(w_hi[n % 2][:, h_ * HALF:h_ * HALF + kts * P], raw[n % 4][:, cols]).then_inc(hi_ready, 1)

            def buffer_free(norm, k):
                if not isinstance(k, int) or (KD - 1) * norm + k >= 2:
                    act.wait_ge(sq_added, (KD - 1) * norm - 1 + k)

            def norm_root(norm, out):
                for t in range(2):
                    cols = slice(t * H, (t + 1) * H)
                    act.wait_ge(stat_done, 2 * norm + t + 1)
                    step.mark(act.activation(out[:, cols], A[t][:, 0:H], ACT.Ln, bias=eps[:], scale=1.0 / D))
                    step.wait(act)
                    act.activation(out[:, cols], out[:, cols], ACT.Exp, scale=-0.5).then_inc(rstd_ready, 1)

            def normed(pre, col, i):
                for e in range(2):
                    k = 2 * i + e
                    buffer_free(2 * pre, k)
                    act.wait_ge(x_new, KD * (pre - 1) + 1 + k)
                    act.activation(h_hi[:, k, :], x[:, k, :], ACT.Copy, scale=vec[:, bass.ds(k + col, 1)]
                                   ).then_inc(h_hi_ready, 1)
                    act.activation(S[e][:], x[:, k, :], ACT.Square).then_inc(sq_ready, 1)

            act.preload_act_table_set("natural_log_exp_and_others")
            act.wait_ge(set_up, 3)
            act.wait_ge(const_in, 64)
            for k in range(KD):
                act.wait_ge(x_in[k], 16)
                act.activation(h_hi[:, k, :], x[:, k, :], ACT.Copy, scale=vec[:, gain_col(MIX_PRE, 0) + k:
                                                                          gain_col(MIX_PRE, 0) + k + 1]
                               ).then_inc(h_hi_ready, 1)
                if k < 4:
                    split(k, 0)
                buffer_free(0, k)
                act.activation(S[k % 2][:], x[:, k, :], ACT.Square).then_inc(sq_ready, 1)

            def exps(s):
                act.wait_ge(p_sum, 2 * s + 3)
                if s < 0:
                    for c in range(2):
                        act.activation(pr_s[:, c, :], pr_s[:, c, :], ACT.Exp, bias=sm_s[:, 0, c:c + 1],
                                       accum_out=sm_s[:, 1, c:c + 1])
                    act.activation(sm_s[:, 3, :], sm_s[:, 2, :], ACT.Exp).then_inc(p_exp, 1)
                    return
                w = slice(WIN, 2 * WIN) if s < 2 else slice(0, 2 * WIN)
                z = sm[:, s % 2]
                for j in range(GRP):
                    act.activation(pr[s % 2][:, j, w], pr[s % 2][:, j, w], ACT.Exp, bias=z[:, 0, j:j + 1],
                                   accum_out=z[:, 1, j:j + 1])
                act.activation(z[:, 3, :], z[:, 2, :], ACT.Exp).then_inc(p_exp, 1)

            def probs_copied(s):
                act.wait_ge(pT_done, s + 2)
                if s < 0:
                    act.copy(pT_s[:].rearrange("p a b -> p (a b)"), A[2][:, 0:2 * P]).then_inc(pT_copied, 1)
                    act.copy(pT_n[:].rearrange("p a b -> p (a b)"), A[3][0:TS, 0:2 * P]).then_inc(pT_copied, 1)
                    return
                if s:
                    act.wait_ge(o_done, s + 1)
                if s < 2:
                    act.copy(pT[:, 1, :], A[3][:]).then_inc(pT_copied, 2)
                    return
                for c in range(2):
                    act.copy(pT[:, c, :], A[2 + c][:]).then_inc(pT_copied, 1)

            def attention_hi(s):
                act.wait_ge(o_done, s + 2)
                if s < 0:
                    for g in range(2):
                        r = slice(64 * g, 64 * g + 64)
                        src = A[2][r, 0:256].rearrange("p (b c) -> p b c", b=NB)[:, :, 16 * g:16 * g + 16]
                        dst = y_hi[r, CA:KD, TP:T].rearrange("p j (b t) -> p b j t", b=NB)
                        i_ = act.copy(dst, src.rearrange("p b (j t) -> p b j t", j=GRP))
                    i_.then_inc(yb_hi, 1)
                    return
                n, g = divmod(s, 2)
                r = slice(64 * g, 64 * g + 64)
                act.copy(y_hi[r, CA:KD, n * WIN:(n + 1) * WIN], A[2][r, :].rearrange("p (j q) -> p j q", j=GRP)
                         ).then_inc(yb_hi, 1)

            extra = {11: [lambda: vT(0), lambda: vT(1)], 12: [lambda: vT(2)], 13: [lambda: exps(-1)],
                     15: [lambda: probs_copied(-1)], 16: [lambda: attention_hi(-1)]}
            for s in range(8):
                extra.setdefault(15 + 2 * s, []).append(lambda s=s: exps(s))
                extra.setdefault(17 + 2 * s, []).append(lambda s=s: probs_copied(s))
                extra.setdefault(18 + 2 * s, []).append(lambda s=s: attention_hi(s))

            def vT(part):
                act.wait_ge(vT_done, part + 1)
                if part == 0:
                    act.copy(vtok[:].rearrange("p a b -> p (a b)"), A[2][:]).then_inc(vT_copied, 1)
                else:
                    b = slice(4 * part - 4, 4 * part)
                    act.copy(vnew[:, b, :].rearrange("p a b -> p (a b)"), A[4 - part][0:TS, :]).then_inc(vT_copied, 1)

            for m in range(36):
                split(m + 4, 0)
                if m == 1:
                    norm_root(0, rstd)
                c, r = divmod(m - 12, 6)
                if m >= 12 and r == 3:
                    act.wait_ge(evac, tile("in_ab", 7 + 3 * c))
                    act.activation(S[1][:], S[3][:], ACT.Copy, scale=vec[:, V_CONVA + 2 * CA + c:V_CONVA + 2 * CA + c + 1]
                                   ).then_inc(tap_ready, 1)
                if m >= 12 and r == 5:
                    act.wait_ge(evac, tile("in_ab", 8 + 3 * c))
                    act.copy(y_hi[:, c, :], S[0][:]).then_inc(g_hi_ready, 1)
                for f in extra.get(m, []):
                    f()
                if m == 12:
                    act.wait_ge(evac, tile("in_ab", 4))
                    act.dma_start(dram["o_kp"], k_sb[:, TP - WIN:TP]).then_inc(stored, 16)
                    act.wait_ge(kc_ready, 1)
                    act.wait_ge(const_a, 64)
                    act.dma_start(dram["o_ks"], kc[:, :, TS:TS + WIN]).then_inc(stored, 16)
                    act.wait_ge(vT_copied, 3)
                    act.dma_start(dram["o_vp"], vtok[:, NBLK - 1, :]).then_inc(stored, 16)
                    act.dma_start(dram["o_vs"][:, 0:WIN - TS, :].rearrange("b k f -> k b f"), vc[TS:WIN, :, :]
                                  ).then_inc(stored, 16)
                    act.dma_start(dram["o_vs"][:, WIN - TS:WIN, :].rearrange("b k f -> k b f"), vnew[:]
                                  ).then_inc(stored, 16)

            def out_tile(count, norm, k, e):
                buffer_free(norm, k)
                act.wait_ge(evac, count)
                act.activation(S[e][:], mix[:, k, :], ACT.Square).then_inc(sq_ready, 1)

            def out_phase(name, norm):
                for k in range(KD):
                    for e in range(2):
                        split(2 * (UNIT0[name] + k) + e + 4, 0)
                    out_tile(tile(name, k), norm, k, k % 2)

            def boundary(post, pre_kind, layer):
                norm_root(post, S[3])
                if post == 3:
                    for to, name in ((masks, "c_masks"), (mask_s, "c_mask_s"), (own, "c_own"), (keep, "c_keep")):
                        act.dma_start(to[:], dram[name]).then_inc(const_c, 16)
                    act.dma_start(S0[:], dram["state0"][0, :, :, :]).then_inc(state0_in, 16)
                pre = (post + 1) // 2
                if pre == 4:
                    return
                with act.Fori(0, KD // 2) as i:
                    normed(pre, gain_col(pre_kind, layer), i)

            out_phase("out_ab", 1)
            boundary(1, FFN_PRE, 0)
            act.wait_ge(stored, 5 * 16)

            def ffn(layer):
                name = f"up{layer}"

                def up(i, s_off, first=False):
                    for u in range(2):
                        pair = CA + KF * layer + u + 2 * i
                        for t in range(4):
                            split(2 * UNIT0[name] + 4 * u + t + 4 + s_off, 8 * i if s_off == 0 else 0)
                            if t == 1 and u == 0 and first:
                                norm_root(2 + 4 * layer, rstd)
                            if t == 1:
                                act.wait_ge(evac, tile(name, 2 * u) + 4 * i)
                                w = V_CONVF + (layer * 3 + 2) * KF
                                act.activation(S[1][:], S[0][:], ACT.Copy, scale=vec[:, bass.ds(w + u + 2 * i, 1)]
                                               ).then_inc(tap_ready, 1)
                            if t == 2:
                                act.wait_ge(conv_done, pair + 1)
                                act.activation(S[2][:], S[1][:], ACT.Gelu_apprx_tanh).then_inc(act_done, 1)
                            if t == 3:
                                act.wait_ge(evac, tile(name, 2 * u + 1) + 4 * i)
                                act.copy(g_hi[:, u + 2 * i, :], S[3][:]).then_inc(g_hi_ready, 1)

                up(0, 0, True)
                act.preload_act_table_set("gelu_apprx_tanh_and_others")
                with act.Fori(1, KF // 2 - 1) as i:
                    up(i, 0)
                up(KF // 2 - 1, 8 * (KF // 2 - 1))
                name = f"down{layer}"

                def down(i, s_off):
                    for e in range(2):
                        for t in range(4):
                            split(2 * UNIT0[name] + 4 * e + t + 4 + s_off, 8 * i if s_off == 0 else 0)
                        out_tile(tile(name, e) + 2 * i, 3 + 4 * layer, 2 * i + e, e)

                with act.Fori(0, KD // 2 - 1) as i:
                    down(i, 0)
                act.preload_act_table_set("natural_log_exp_and_others")
                down(KD // 2 - 1, 8 * (KD // 2 - 1))
                boundary(3 + 4 * layer, MIX_PRE, 1)

            ffn(0)

            act.wait_ge(C["lb_ready"], 1)
            act.activation(lb[:, 1:3, :], lb[:, 1:3, :], ACT.Exp).then_inc(C["lb_done"], 1)

            STEPS_C = 6

            def hgrn_tick(t, prev, cur):
                if prev is not None:
                    if t == 0:
                        act.wait_ge(C["gn_ready"], prev + 1)
                        step.mark(act.activation(sg[:], sg[:], ACT.Exp, scale=-1.0))
                        step.wait(act)
                        step.mark(act.activation(sg[:], sg[:], ACT.Ln, bias=1.0))
                        step.wait(act)
                        act.activation(sg[:], sg[:], ACT.Exp, scale=-1.0).then_inc(C["sg_ready"], 1)
                    if t == 1:
                        act.wait_ge(C["snew_ready"], 2 * prev + 2)
                        act.dma_start(dram["o_ss"][prev, :, :, :], Snew[:]).then_inc(state_out, 16)
                        act.dma_start(dram["o_sp"][prev, :, :], Sst[:, NCH - 1, :]).then_inc(state_out, 16)
                    if t == 3:
                        act.wait_ge(C["oc_done"], prev + 1)
                        act.activation(S[2][:, 0:TP], A[3][:], ACT.Square)
                        act.activation(S[2][:, TP:T], A[2][:, 0:NB * TS], ACT.Square).then_inc(C["osq_ready"], 1)
                        if cur is not None:
                            act.wait_ge(C["s0_scaled"], prev + 1)
                            act.dma_start(S0[:], dram["state0"][cur, :, :, :]).then_inc(state0_in, 16)
                    if t == 4:
                        act.wait_ge(C["ostat_done"], prev + 1)
                        for z in range(2):
                            step.mark(act.activation(S[3][:, z * H:(z + 1) * H], A[z][:, 0:H], ACT.Ln, bias=eps[:],
                                                       scale=1.0 / P))
                        step.wait(act)
                        act.activation(S[3][:], S[3][:], ACT.Exp, scale=-0.5).then_inc(C["ors_ready"], 1)
                if cur is not None:
                    if t == 1:
                        act.wait_ge(C["fl_ready"], cur + 1)
                        step.mark(act.activation(S[0][:], S[0][:], ACT.Exp, scale=-1.0))
                        step.wait(act)
                        step.mark(act.activation(S[1][:], S[0][:], ACT.Ln, bias=1.0))
                        step.wait(act)
                        act.activation(S[1][:], S[1][:], ACT.Exp, scale=-1.0).then_inc(C["sig_ready"], 1)
                    if t == 2:
                        act.wait_ge(C["ff_ready"], cur + 1)
                        act.activation(S[1][:], S[1][:], ACT.Ln).then_inc(C["lf_ready"], 1)
                    if t == 3:
                        act.wait_ge(C["G_ready"], cur + 1)
                        act.activation(eG[:], G[:], ACT.Exp).then_inc(C["eG_ready"], 1)
                        act.wait_ge(C["kd_diff"], cur + 1)
                        act.activation(kd[:], kd[:], ACT.Exp).then_inc(C["kd_exp"], 1)
                    if t == 5:
                        act.wait_ge(C["kdT_done"], cur + 1)
                        act.copy(kt[:].rearrange("p a b -> p (a b)"), A[0][:])
                        act.copy(kt_s[:], A[1][0:NB * TS, 0:P]).then_inc(C["kdT_copied"], 1)
                if prev is not None and t == 5:
                    act.wait_ge(C["oy_ready"], prev + 1)
                    act.copy(y_hi[:, prev, :], S[3][:]).then_inc(C["oy_hi"], 1)
                if cur is not None:
                    if 4 <= t <= 7:
                        l = t - 4
                        act.wait_ge(C["lev_diff"], 4 * cur + l + 1)
                        v = lev[l][:].rearrange("p (n a s) -> p n a s", a=2, s=SPANS[l])
                        act.activation(v[:, :, 0, :], v[:, :, 0, :], ACT.Exp, scale=-1.0)
                        act.activation(v[:, :, 1, :], v[:, :, 1, :], ACT.Exp).then_inc(C["lev_exp"], 1)
                    if t == 6:
                        act.wait_ge(C["diag_diff"], cur + 1)
                        act.activation(E1[:], E2[:], ACT.Exp)
                        act.activation(E2[:], E2[:], ACT.Exp, scale=-1.0).then_inc(C["diag_exp"], 1)
                        act.wait_ge(C["vcT_done"], cur + 1)
                        act.copy(vt[:].rearrange("p a b -> p (a b)"), A[0][:])
                        act.copy(vt_s[:], A[1][0:NB * TS, 0:P]).then_inc(C["vcT_copied"], 1)

            def head(hd, prev, s_off):
                for t in range(8):
                    split(2 * UNIT0["in_c"] + t + 4 + s_off, 8 * hd if s_off == 0 else 0)
                    if isinstance(hd, int) and hd == 0 and t == 1:
                        norm_root(4, rstd)
                    hgrn_tick(t, prev, hd)

            head(0, None, 0)
            base = step.n
            with act.Fori(1, HEADS - 1) as hd:
                step.n = base + STEPS_C * (hd - 1)
                head(hd, hd - 1, 0)
            step.n = base + STEPS_C * (HEADS - 2)
            head(HEADS - 1, HEADS - 2, 8 * (HEADS - 1))
            assert step.n == base + STEPS_C * (HEADS - 1), step.n - base
            for t in range(6):
                hgrn_tick(t, HEADS - 1, None)
            out_phase("out_c", 5)
            boundary(5, FFN_PRE, 1)
            act.wait_ge(state_out, 32 * HEADS)
            ffn(1)

        @block.vector
        def _(dve):
            step = Steps(dve_step)

            def split(m, off):
                s = m + off if isinstance(off, int) else m
                if s >= 2 * UNITS:
                    return
                n, h_, kt0, kts = half_of(s)
                dve.wait_ge(hi_ready, m + 1 + off)
                cols, to = slice(kt0 * P, (kt0 + kts) * P), slice(h_ * HALF, h_ * HALF + kts * P)
                dve.tensor_tensor(w_lo[n % 2][:, to], raw[n % 4][:, cols], w_hi[n % 2][:, to], ALU.subtract
                                  ).then_inc(lo_ready, 1)

            def col(c, k):
                return vec[:, c + k:c + k + 1] if isinstance(k, int) else vec[:, bass.ds(k + c, 1)]

            def h_lo_tile(pre, k, c):
                dve.wait_ge(h_hi_ready, KD * pre + 1 + k)
                dve.scalar_tensor_tensor(h_lo[:, k, :], x[:, k, :], col(c, k), h_hi[:, k, :], ALU.mult, ALU.subtract
                                         ).then_inc(h_ready, 1)

            def conv(src, w0, w1, count, sample_count):
                dve.wait_ge(tap_ready, count + 1)
                dve.wait_ge(sp_ready, sample_count + 1)
                y = S[1]
                ys = sample(y[:, TP:T])
                step.mark(dve.scalar_tensor_tensor(y[:, 1:TP], src[:, 0:TP - 1], w1, y[:, 1:TP], ALU.mult, ALU.add))
                step.mark(dve.scalar_tensor_tensor(ys, sp[:, :, 1:1 + TS], w1, ys, ALU.mult, ALU.add))
                step.wait(dve)
                dve.scalar_tensor_tensor(y[:, 2:TP], src[:, 0:TP - 2], w0, y[:, 2:TP], ALU.mult, ALU.add)
                dve.scalar_tensor_tensor(ys, sp[:, :, 0:TS], w0, ys, ALU.mult, ALU.add).then_inc(conv_done, 1)

            dve.wait_ge(const_in, 64)
            for k in range(KD):
                h_lo_tile(0, k, gain_col(MIX_PRE, 0))
                if k < 4:
                    split(k, 0)

            def lower_bounds_a():
                l0, l1 = [vec[:, V_LB + HEADS * i:V_LB + HEADS * (i + 1)] for i in range(2)]
                step.mark(dve.tensor_tensor(lb[:, 0, :], l0, l1, ALU.max))
                step.wait(dve)
                dve.tensor_tensor(lb[:, 1, :], l0, lb[:, 0, :], ALU.subtract)
                dve.tensor_tensor(lb[:, 2, :], l1, lb[:, 0, :], ALU.subtract).then_inc(C["lb_ready"], 1)

            def lower_bounds_b():
                dve.wait_ge(C["lb_done"], 1)
                step.mark(dve.tensor_tensor(lb[:, 3, :], lb[:, 1, :], lb[:, 2, :], ALU.add))
                step.wait(dve)
                step.mark(dve.reciprocal(lb[:, 4, :], lb[:, 3, :]))
                step.wait(dve)
                dve.tensor_tensor(lb[:, 5, :], lb[:, 1, :], lb[:, 4, :], ALU.mult)
                step.mark(dve.tensor_tensor(lb[:, 6, :], lb[:, 2, :], lb[:, 4, :], ALU.mult))
                step.wait(dve)
                step.mark(dve.tensor_tensor(lb[:, 6, :], lb[:, 5, :], lb[:, 6, :], ALU.add))
                step.wait(dve)
                step.mark(dve.tensor_tensor(lb[:, 6, :], lb[:, 6, :], lb[:, 5, :], ALU.subtract))
                step.wait(dve)
                step.mark(dve.tensor_scalar(lb[:, 6, :], lb[:, 6, :], 0.0, 1.0, ALU.max, ALU.min))
                step.wait(dve)
                step.mark(dve.tensor_scalar(lb[:, 7, :], lb[:, 6, :], -1.0, 1.0, ALU.mult, ALU.add))

            def softmax_in(s):
                dve.wait_ge(s_done, s + 2)
                dve.wait_ge(const_a, 64)
                if s < 0:
                    for c in range(2):
                        dve.tensor_tensor(pr_s[:, c, :], A[c][:, 0:WIN + TS], bias_s[:], ALU.add).then_inc(s_biased, 1)
                    view, sink = pr_s[:], vec[:, V_SINKS:V_SINKS + 1].broadcast_to([P, 2])
                    z = sm_s
                else:
                    g = s % 2
                    w = slice(WIN, 2 * WIN) if s < 2 else slice(0, 2 * WIN)
                    if s >= 2:
                        dve.wait_ge(pT_done, s)
                    for a in range(2):
                        dve.tensor_tensor(pr[g][:, 2 * a:2 * a + 2, w],
                                          A[a][:].rearrange("p (j k) -> p j k", j=2)[:, :, w],
                                          bias[:, 4 * g + 2 * a:4 * g + 2 * a + 2, w], ALU.add).then_inc(s_biased, 1)
                    view, sink = pr[g][:, :, w], vec[:, V_SINK + 4 * g:V_SINK + 4 * g + 4]
                    z = sm[:, g]
                dve.wait_ge(s_biased, 2 * s + 4)
                step.mark(dve.tensor_reduce(z[:, 4, :], view, AX_X, ALU.max))
                step.wait(dve)
                step.mark(dve.tensor_tensor(z[:, 5, :], z[:, 4, :], sink, ALU.max))
                step.wait(dve)
                dve.tensor_scalar(z[:, 0, :], z[:, 5, :], -1.0, None, ALU.mult)
                dve.tensor_tensor(z[:, 2, :], sink, z[:, 5, :], ALU.subtract).then_inc(p_sum, 1)

            def softmax_sum(s):
                z = sm_s if s < 0 else sm[:, s % 2]
                dve.wait_ge(p_exp, s + 2)
                step.mark(dve.tensor_tensor(z[:, 4, :], z[:, 1, :], z[:, 3, :], ALU.add))
                step.wait(dve)
                dve.reciprocal(z[:, 5, :], z[:, 4, :]).then_inc(p_sum, 1)

            def attention_lo(s):
                dve.wait_ge(yb_hi, s + 2)
                if s < 0:
                    for g in range(2):
                        r = slice(64 * g, 64 * g + 64)
                        src = A[2][r, 0:256].rearrange("p (b c) -> p b c", b=NB)[:, :, 16 * g:16 * g + 16]
                        src = src.rearrange("p b (j t) -> p b j t", j=GRP)
                        hi, lo = [y[r, CA:KD, TP:T].rearrange("p j (b t) -> p b j t", b=NB) for y in (y_hi, y_lo)]
                        i_ = dve.tensor_tensor(lo, src, hi, ALU.subtract)
                    i_.then_inc(yb_lo, 1)
                    return
                n, g = divmod(s, 2)
                r, c = slice(64 * g, 64 * g + 64), slice(n * WIN, (n + 1) * WIN)
                dve.tensor_tensor(y_lo[r, CA:KD, c], A[2][r, :].rearrange("p (j q) -> p j q", j=GRP),
                                  y_hi[r, CA:KD, c], ALU.subtract).then_inc(yb_lo, 1)

            extra = {12: [lambda: softmax_in(-1)], 13: [lambda: softmax_sum(-1)], 16: [lambda: attention_lo(-1)]}
            for s in range(8):
                extra.setdefault(14 + 2 * s, []).append(lambda s=s: softmax_in(s))
                extra.setdefault(15 + 2 * s, []).append(lambda s=s: softmax_sum(s))
                extra.setdefault(18 + 2 * s, []).append(lambda s=s: attention_lo(s))

            lower_bounds_a()
            for m in range(36):
                split(m + 4, 0)
                u = m // 2
                if m % 2:
                    dve.wait_ge(half_done, m + 1)
                    if u == 0:
                        dve.wait_ge(rstd_ready, 2)
                    src, r2 = acc_v[u % 2], tok2(rstd[:])
                    c, r = divmod(u - 6, 3)
                    if u < 4:
                        dve.scalar_tensor_tensor(tok2(q_sb[:, u, :]), src, HD ** -0.5, r2, ALU.mult, ALU.mult
                                                 ).then_inc(evac, 1)
                    elif u < 6:
                        dve.tensor_tensor(tok2((k_sb, v_sb)[u - 4][:]), src, r2, ALU.mult).then_inc(evac, 1)
                    elif r == 0:
                        if c:
                            dve.wait_ge(g_ready, c)
                        dve.tensor_tensor(tok2(S[0][:]), src, r2, ALU.mult).then_inc(evac, 1)
                    elif r == 1:
                        dve.wait_ge(gate_ready, 2 * c + 1)
                        dve.tensor_tensor(tok2(S[3][:]), src, tok2(S[0][:]), ALU.mult).then_inc(evac, 1)
                    else:
                        dve.wait_ge(gate_ready, 2 * c + 2)
                        dve.tensor_tensor(tok2(S[0][:]), src, tok2(S[1][:]), ALU.mult).then_inc(evac, 1)
                if m >= 12 and (m - 12) % 6 == 4:
                    c = (m - 12) // 6
                    conv(S[3], col(V_CONVA, c), col(V_CONVA + CA, c), c, c)
                for f in extra.get(m, []):
                    f()
                if m >= 12 and (m - 12) % 6 == 5:
                    c = (m - 12) // 6
                    dve.wait_ge(g_hi_ready, c + 1)
                    dve.tensor_tensor(y_lo[:, c, :], S[0][:], y_hi[:, c, :], ALU.subtract).then_inc(g_ready, 1)

            def out_tile(u_done, out, k):
                dve.wait_ge(half_done, u_done)
                dve.tensor_copy(tok2(mix[:, k, :]), acc_v[out]).then_inc(evac, 1)

            def out_phase(name):
                for k in range(KD):
                    for e in range(2):
                        split(2 * (UNIT0[name] + k) + e + 4, 0)
                    out_tile(2 * (UNIT0[name] + k) + 2, k % 2, k)

            def boundary(post, layer, pre_kind, pre_layer):
                dve.wait_ge(rstd_ready, 2 * (post + 1))
                pre = (post + 1) // 2
                pg = gain_col(MIX_POST if post % 4 == 1 else FFN_POST, layer)

                def add(k):
                    dve.scalar_tensor_tensor(x[:, k, :], mix[:, k, :], col(pg, k), x[:, k, :], ALU.mult, ALU.add
                                             ).then_inc(x_new, 1)

                def lo(k):
                    if pre < 4:
                        h_lo_tile(pre, k, gain_col(pre_kind, pre_layer))

                def tile_pair(i):
                    step.mark(dve.tensor_tensor(mix[:, 2 * i, :], mix[:, 2 * i, :], S[3][:], ALU.mult))
                    if not isinstance(i, int):
                        lo(2 * i - 1)
                    step.wait(dve)
                    add(2 * i)
                    dve.wait_ge(mix_scaled, KD // 2 * (pre - 1) + 1 + i)
                    add(2 * i + 1)
                    lo(2 * i)

                tile_pair(0)
                base = step.n
                with dve.Fori(1, KD // 2) as i:
                    step.n = base + i - 1
                    tile_pair(i)
                step.n = base + KD // 2 - 1
                lo(KD - 1)

            out_phase("out_ab")
            boundary(1, 0, FFN_PRE, 0)

            def ffn(layer):
                name = f"up{layer}"

                def up(i, s_off, first=False):
                    for u in range(2):
                        j = u + 2 * i
                        pair = CA + KF * layer + j
                        w = V_CONVF + layer * 3 * KF
                        for t in range(4):
                            split(2 * UNIT0[name] + 4 * u + t + 4 + s_off, 8 * i if s_off == 0 else 0)
                            if t == 1:
                                dve.wait_ge(half_done, 2 * UNIT0[name] + 4 * u + 2 + 8 * i)
                                if first and u == 0:
                                    dve.wait_ge(rstd_ready, 2 * (3 + 4 * layer))
                                dve.wait_ge(sp_ready, pair)
                                dve.tensor_tensor(tok2(S[0][:]), acc_v[0], tok2(rstd[:]), ALU.mult).then_inc(evac, 1)
                            if t == 2:
                                conv(S[0], col(w, j), col(w + KF, j), pair, pair)
                            if t == 3:
                                dve.wait_ge(half_done, 2 * UNIT0[name] + 4 * u + 4 + 8 * i)
                                dve.wait_ge(gate_ready, pair + CA + 1)
                                dve.tensor_tensor(tok2(S[3][:]), acc_v[1], tok2(S[2][:]), ALU.mult).then_inc(evac, 1)
                                dve.wait_ge(g_hi_ready, pair + 1)
                                dve.tensor_tensor(g_lo[:, j, :], S[3][:], g_hi[:, j, :], ALU.subtract
                                                  ).then_inc(g_ready, 1)

                base = step.n
                up(0, 0, True)
                per = step.n - base
                base = step.n
                with dve.Fori(1, KF // 2 - 1) as i:
                    step.n = base + per * (i - 1)
                    up(i, 0)
                step.n = base + per * (KF // 2 - 2)
                up(KF // 2 - 1, 8 * (KF // 2 - 1))
                name = f"down{layer}"

                def down(i, s_off):
                    for e in range(2):
                        for t in range(4):
                            split(2 * UNIT0[name] + 4 * e + t + 4 + s_off, 8 * i if s_off == 0 else 0)
                        out_tile(2 * UNIT0[name] + 4 * e + 4 + 8 * i, e, 2 * i + e)

                with dve.Fori(0, KD // 2 - 1) as i:
                    down(i, 0)
                down(KD // 2 - 1, 8 * (KD // 2 - 1))
                boundary(3 + 4 * layer, layer, MIX_PRE, 1)

            ffn(0)

            def level_ops(l, cur):
                v = lev[l][:].rearrange("p (n s) -> p n s", s=2 * SPANS[l])
                g = G[:, 0:TP].rearrange("p (n s) -> p n s", s=2 * SPANS[l])
                mid = g[:, :, SPANS[l] - 1:SPANS[l]].broadcast_to([P, TP // (2 * SPANS[l]), 2 * SPANS[l]])
                dve.tensor_tensor(v, g, mid, ALU.subtract).then_inc(C["lev_diff"], 1)

            def level_q(l, cur):
                dve.wait_ge(C["lev_exp"], 4 * cur + l + 1)
                v, q = [z.rearrange("p (n a s) -> p n a s", a=2, s=SPANS[l]) for z in (lev[l][:], qn[:, 0:TP])]
                dve.tensor_tensor(v[:, :, 1, :], v[:, :, 1, :], q[:, :, 1, :], ALU.mult).then_inc(C["lev_ready"], 1)

            def came(b, which):
                dve.tensor_copy(arrival[0:NB * TS, which:which + 1], A[b][0:NB * TS, 0:1])

            def take_level(prev, which):
                b = (1, 2, 3, 0, 1)[which]
                order = (0, 2, 3, 4, 5)[which]
                dve.wait_ge(C["al_done"], 6 * prev + order + 1)
                if order:
                    dve.wait_ge(C["al_taken"], 6 * prev + order)
                came(b, which)
                if which == 0:
                    at, al = [z[:].rearrange("p (c t) -> p c t", c=NCH) for z in (AT, A[b])]
                    mask = masks[:, 0:1, :].broadcast_to([P, NCH, CH])
                else:
                    span = SPANS[which - 1]
                    n = CH // (2 * span)
                    at = later(AT[:], span).rearrange("p (c n) s -> p c n s", c=NCH)
                    al = A[b][:, 0:TP // 2].rearrange("p (c n s) -> p c n s", c=NCH, s=span)
                    mask = later(masks[:, which, :], span).rearrange("p (c n) s -> p c n s", c=1)
                    mask = mask.broadcast_to([P, NCH, n, span])
                dve.copy_predicated(at, mask, al).then_inc(C["al_taken"], 1)

            def head_out(t, cur):
                u = t // 2
                dve.wait_ge(half_done, 2 * UNIT0["in_c"] + t + 1 + 8 * cur)
                if isinstance(cur, int) and cur == 0 and t == 1:
                    dve.wait_ge(rstd_ready, 10)
                out = (S[0], qn, vv, gn)[u]
                dve.tensor_tensor(tok2(out[:]), acc_v[u % 2], tok2(rstd[:]), ALU.mult).then_inc(evac, 1)
                if t == 1:
                    dve.wait_ge(evac, tile("in_c", 0) + 4 * cur)
                    dve.tensor_scalar(S[0][:], S[0][:], -80.0, None, ALU.max).then_inc(C["fl_ready"], 1)
                if t == 7:
                    dve.wait_ge(evac, tile("in_c", 3) + 4 * cur)
                    dve.tensor_scalar(sg[:], gn[:], -80.0, None, ALU.max).then_inc(C["gn_ready"], 1)

            def hgrn_tick(t, prev, cur):
                if prev is not None:
                    if t == 0:
                        dve.wait_ge(C["s0_scaled"], prev + 1)
                        dve.wait_ge(C["us_done"], 2 * prev + 1)
                        dve.tensor_tensor(Snew[:, 0:4, :], Snew[:, 0:4, :], A[3][:].rearrange("p (a b) -> p a b", a=4),
                                          ALU.add).then_inc(C["snew_ready"], 1)
                        dve.wait_ge(C["us_done"], 2 * prev + 2)
                        dve.tensor_tensor(Snew[:, 4:8, :], Snew[:, 4:8, :], A[0][:].rearrange("p (a b) -> p a b", a=4),
                                          ALU.add).then_inc(C["snew_ready"], 1)
                        take_level(prev, 0)
                        dve.wait_ge(C["al_done"], 6 * prev + 2)
                        came(2, 5)
                        dve.copy_predicated(AT_s[:], mask_s[:], A[2][0:NB * TS, 0:NB * TS]).then_inc(C["al_taken"], 1)
                    if t == 1:
                        take_level(prev, 1)
                        take_level(prev, 2)
                    if t == 2:
                        take_level(prev, 3)
                        take_level(prev, 4)
                    if t == 4:
                        dve.wait_ge(C["osq_ready"], prev + 1)
                        dve.wait_ge(C["gs_ready"], prev + 1)
                        dve.scalar_tensor_tensor(sg[:, 0:TP], A[3][:], vec[:, V_NG:V_NG + 1], sg[:, 0:TP],
                                                 ALU.mult, ALU.mult)
                        dve.scalar_tensor_tensor(sg[:, TP:T], A[2][:, 0:NB * TS], vec[:, V_NG:V_NG + 1],
                                                 sg[:, TP:T], ALU.mult, ALU.mult).then_inc(C["og_ready"], 1)
                    if t == 5:
                        dve.wait_ge(C["ors_ready"], prev + 1)
                        dve.wait_ge(C["og_ready"], prev + 1)
                        dve.tensor_tensor(S[3][:], S[3][:], sg[:], ALU.mult).then_inc(C["oy_ready"], 1)
                        if cur is not None:
                            level_ops(2, cur)
                        dve.wait_ge(C["oy_hi"], prev + 1)
                        dve.tensor_tensor(y_lo[:, prev, :], S[3][:], y_hi[:, prev, :], ALU.subtract
                                          ).then_inc(C["oy_lo"], 1)
                if cur is None:
                    return
                if t == 2:
                    dve.wait_ge(C["sig_ready"], cur + 1)
                    one_lb = lb[:, 7, cur:cur + 1] if isinstance(cur, int) else lb[:, 7, bass.ds(cur, 1)]
                    low = lb[:, 6, cur:cur + 1] if isinstance(cur, int) else lb[:, 6, bass.ds(cur, 1)]
                    dve.scalar_tensor_tensor(kk[:], S[0][:], one_lb, S[1][:], ALU.mult, ALU.mult)
                    step.mark(dve.tensor_scalar(S[1][:], S[1][:], one_lb, low, ALU.mult, ALU.add))
                    step.wait(dve)
                    dve.tensor_scalar(S[1][:], S[1][:], F_FLOOR, None, ALU.max).then_inc(C["ff_ready"], 1)
                    dve.wait_ge(C["lf_ready"], cur + 1)
                    dve.tensor_tensor_scan(G[:], keep[:], S[1][:], 0.0, ALU.mult, ALU.add).then_inc(C["G_ready"], 1)
                if t == 3:
                    dve.wait_ge(C["G_ready"], cur + 1)
                    gp, gs_ = G[:, 0:TP].rearrange("p (c s) -> p c s", c=NCH), sample(G[:, TP:T])
                    dve.tensor_tensor(kd[:, 0:TP].rearrange("p (c s) -> p c s", c=NCH),
                                      gp[:, :, CH - 1:CH].broadcast_to([P, NCH, CH]), gp, ALU.subtract)
                    dve.tensor_tensor(sample(kd[:, TP:T]), gs_[:, :, TS - 1:TS].broadcast_to([P, NB, TS]), gs_,
                                      ALU.subtract).then_inc(C["kd_diff"], 1)
                    level_ops(0, cur)
                if t == 4:
                    level_ops(1, cur)
                    level_q(0, cur)
                if t == 5:
                    if prev is None:
                        level_ops(2, cur)
                    gp, gs_ = G[:, 0:TP].rearrange("p (c s) -> p c s", s=8), sample(G[:, TP:T])
                    dve.tensor_tensor(E2[:, 0:TP].rearrange("p (c s) -> p c s", s=8), gp,
                                      gp[:, :, 3:4].broadcast_to([P, TP // 8, 8]), ALU.subtract)
                    dve.tensor_tensor(sample(E2[:, TP:T]), gs_, gs_[:, :, 1:2].broadcast_to([P, NB, TS]),
                                      ALU.subtract).then_inc(C["diag_diff"], 1)
                    level_q(1, cur)
                if t == 6:
                    level_ops(3, cur)
                    level_q(2, cur)
                    dve.wait_ge(C["vcT_copied"], cur + 1)
                    dve.tensor_tensor(vbd[:], vt_s[:].rearrange("p (a b) -> p a b", a=1).broadcast_to([NB * TS, NB, P]),
                                      own[:], ALU.mult).then_inc(C["vbd_ready"], 1)
                    dve.wait_ge(C["diag_exp"], cur + 1)
                    dve.tensor_tensor(E2[:], E2[:], kk[:], ALU.mult).then_inc(C["diag_ready"], 1)
                if t == 7:
                    level_q(3, cur)
                    dve.wait_ge(C["u_done"], cur + 1)
                    if prev is not None:
                        dve.wait_ge(state_out, 32 * prev + 32)
                    step.mark(dve.tensor_copy(Sst[:, 0, :], A[2][:, 0:P]))
                    for c in range(1, NCH):
                        step.wait(dve)
                        i_ = dve.scalar_tensor_tensor(Sst[:, c, :], Sst[:, c - 1, :],
                                                      eG[:, (c + 1) * CH - 1:(c + 1) * CH],
                                                      A[2][:, c * P:(c + 1) * P], ALU.mult, ALU.add)
                        if c < NCH - 1:
                            step.mark(i_)
                    i_.then_inc(C["st_ready"], 1)

            def head(hd, prev, s_off):
                for t in range(8):
                    if t % 2:
                        head_out(t, hd)
                    split(2 * UNIT0["in_c"] + t + 4 + s_off, 8 * hd if s_off == 0 else 0)
                    hgrn_tick(t, prev, hd)

            lower_bounds_b()
            step.wait(dve)
            dve.wait_ge(const_c, 64)
            dve.wait_ge(set_up, 5)
            head(0, None, 0)
            base, STEPS_C = step.n, 4
            with dve.Fori(1, HEADS - 1) as hd:
                step.n = base + STEPS_C * (hd - 1)
                head(hd, hd - 1, 0)
            step.n = base + STEPS_C * (HEADS - 2)
            head(HEADS - 1, HEADS - 2, 8 * (HEADS - 1))
            assert step.n == base + STEPS_C * (HEADS - 1), step.n - base
            for t in range(6):
                hgrn_tick(t, HEADS - 1, None)
            out_phase("out_c")
            boundary(5, 1, FFN_PRE, 1)
            ffn(1)

        @block.gpsimd
        def _(pool):
            pool.memset(ones[:], 1.0).then_inc(set_up, 1)
            pool.memset(eps[:], EPS).then_inc(set_up, 1)
            pool.memset(qbd[:], 0.0).then_inc(set_up, 1)
            step = Steps(pool_step)

            def add_squares(norm, post=False):
                def scale(i):
                    k = 2 * i + 1
                    pool.tensor_tensor(mix[:, k, :], mix[:, k, :], S[3][:], ALU.mult).then_inc(mix_scaled, 1)

                def add(k):
                    pool.wait_ge(sq_ready, KD * norm + 1 + k)
                    pool.wait_ge(sq_added, (KD - 1) * norm + k)
                    e = k % 2 if isinstance(k, int) else 0
                    pool.tensor_tensor(S[2][:], S[2][:], S[e][:], ALU.add).then_inc(sq_added, 1)

                if post:
                    pool.wait_ge(rstd_ready, 2 * norm)
                    scale(0)
                    scale(1)
                if norm < 8:
                    if norm:
                        pool.wait_ge(stat_done, 2 * norm)
                    pool.wait_ge(sq_ready, KD * norm + 2)
                    pool.tensor_tensor(S[2][:], S[0][:], S[1][:], ALU.add).then_inc(sq_added, 2)
                if post:
                    scale(2)
                if norm < 8:
                    add(2)
                    add(3)
                if post:
                    scale(3)
                if norm < 8:
                    add(4)
                    add(5)
                    add(6)

            def conv_side(src, state, tail, count, input_out):
                pool.wait_ge(evac, input_out)
                if not isinstance(count, int) or count:
                    pool.wait_ge(conv_done, count)
                step.mark(pool.tensor_copy(sp[:, :, 0:2], state()))
                step.mark(pool.tensor_copy(sp[:, :, 2:2 + TS], sample(src[:, TP:T])))
                step.wait(pool)
                step.mark(pool.tensor_copy(tail(), src[:, TP - 2:TP]))
                pool.tensor_copy(state(), sp[:, :, TS:TS + 2]).then_inc(sp_ready, 1)

            add_squares(0)
            pool.wait_ge(const_in, 64)
            pool.wait_ge(evac, tile("in_ab", 3))
            pool.wait_ge(set_up, 3)
            for g in range(2):
                r = slice(64 * g, 64 * g + 64)
                if g:
                    pool.wait_ge(qbd_ready, 1)
                pool.tensor_copy(qbd[r, :, 16 * g:16 * g + 16].rearrange("p b (j t) -> p j b t", j=GRP),
                                 q_sb[r, :, TP:T].rearrange("p j (b t) -> p j b t", b=NB)).then_inc(qbd_ready, 1)
            pool.wait_ge(evac, tile("in_ab", 4))
            pool.wait_ge(qbd_ready, 2)
            pool.tensor_copy(kc[:, :, WIN:WIN + TS], sample(k_sb[:, TP:T])).then_inc(kc_ready, 1)

            def normalise(s):
                pool.wait_ge(p_sum, 2 * s + 4)
                if s < 0:
                    z = sm_s[:, 5, :].rearrange("p (c a) -> p c a", a=1).broadcast_to([P, 2, WIN + TS])
                    pool.tensor_tensor(pr_s[:], pr_s[:], z, ALU.mult).then_inc(p_ready, 1)
                    return
                w = slice(WIN, 2 * WIN) if s < 2 else slice(0, 2 * WIN)
                p = pr[s % 2][:, :, w]
                z = sm[:, s % 2, 5, :].rearrange("p (c a) -> p c a", a=1).broadcast_to([P, GRP, 128 if s < 2 else 256])
                pool.tensor_tensor(p, p, z, ALU.mult).then_inc(p_ready, 1)

            steps_of = {13: [-1]}
            for s in range(8):
                steps_of.setdefault(15 + 2 * s, []).append(s)
            for m in range(12, 36):
                c, r = divmod(m - 12, 6)
                if r == 1:
                    pool.wait_ge(evac, tile("in_ab", 6 + 3 * c))
                    pool.tensor_tensor(S[0][:], S[0][:], rstd[:], ALU.mult).then_inc(gate_ready, 1)
                if r == 3:
                    conv_side(S[3], lambda: st_a[:, c, :, :], lambda: tail_a[:, c, :], c, tile("in_ab", 7 + 3 * c))
                if r == 4:
                    pool.wait_ge(conv_done, c + 1)
                    pool.tensor_tensor(S[1][:], S[1][:], rstd[:], ALU.mult).then_inc(gate_ready, 1)
                for s in steps_of.get(m, []):
                    normalise(s)
            add_squares(1)
            add_squares(2, post=True)

            def ffn(layer):
                base = step.n
                with pool.Fori(0, KF) as j:
                    step.n = base + 3 * j
                    pair = CA + KF * layer + j
                    conv_side(S[0], lambda: st_f[:, layer, j, :, :], lambda: tail_f[:, layer, j, :], pair,
                              tile(f"up{layer}", 0) + 2 * j)
                    pool.wait_ge(act_done, KF * layer + j + 1)
                    pool.tensor_tensor(S[2][:], S[2][:], rstd[:], ALU.mult).then_inc(gate_ready, 1)
                step.n = base + 3 * KF
                pool.wait_ge(evac, tile(f"up{layer}", 2 * KF - 1))
                add_squares(3 + 4 * layer)
                add_squares(4 + 4 * layer, post=True)

            ffn(0)

            def hgrn(prev, cur):
                if prev is not None:
                    pool.wait_ge(C["sg_ready"], prev + 1)
                    pool.tensor_tensor(sg[:], sg[:], gn[:], ALU.mult).then_inc(C["gs_ready"], 1)
                if cur is not None:
                    pool.wait_ge(C["kd_exp"], cur + 1)
                    pool.tensor_tensor(kd[:], kd[:], kk[:], ALU.mult).then_inc(C["kd_ready"], 1)
                if cur is not None:
                    for l in range(3):
                        key_level(l, cur)
                        if l == 0:
                            if prev is not None:
                                pool.wait_ge(C["oc_done"], prev + 1)
                            pool.wait_ge(C["eG_ready"], cur + 1)
                            pool.wait_ge(evac, tile("in_c", 1) + 4 * cur)
                            pool.tensor_tensor(qG[:], eG[:], qn[:], ALU.mult).then_inc(C["qG_ready"], 1)
                    pool.wait_ge(C["diag_exp"], cur + 1)
                    pool.tensor_tensor(E1[:], E1[:], qn[:], ALU.mult).then_inc(C["diag_ready"], 1)
                    pool.wait_ge(state0_in, 16 * cur + 16)
                    if prev is not None:
                        pool.wait_ge(state_out, 32 * prev + 32)
                    e = sample(eG[:, TP:T])[:, :, TS - 1:TS].broadcast_to([P, NB, P])
                    pool.tensor_tensor(Snew[:], S0[:], e, ALU.mult).then_inc(C["s0_scaled"], 1)
                    key_level(3, cur)

            def key_level(l, cur):
                pool.wait_ge(C["lev_exp"], 4 * cur + l + 1)
                v, k_ = [z.rearrange("p (n a s) -> p n a s", a=2, s=SPANS[l]) for z in (lev[l][:], kk[:, 0:TP])]
                pool.tensor_tensor(v[:, :, 0, :], v[:, :, 0, :], k_[:, :, 0, :], ALU.mult).then_inc(C["lev_ready"], 1)

            pool.wait_ge(half_done, 2 * UNIT0["in_c"])
            pool.memset(AT[:], 0.0).then_inc(set_up, 1)
            pool.memset(AT_s[:], 0.0).then_inc(set_up, 1)
            hgrn(None, 0)
            with pool.Fori(1, HEADS) as hd:
                hgrn(hd - 1, hd)
            hgrn(HEADS - 1, None)
            pool.wait_ge(C["osq_ready"], HEADS)
            pool.wait_ge(C["ostat_done"], HEADS)
            add_squares(5)
            add_squares(6, post=True)
            ffn(1)

            pool.wait_ge(sp_ready, CA + 2 * KF)
            step.wait(pool)
            pool.dma_start(dram["o_ca"], tail_a[:]).then_inc(stored_late, 16)
            pool.dma_start(dram["o_cs"], st_a[:]).then_inc(stored_late, 16)
            pool.dma_start(dram["o_fp"], tail_f[:]).then_inc(stored_late, 16)
            pool.dma_start(dram["o_fs"], st_f[:]).then_inc(stored_late, 16)
            pool.wait_ge(stored, 16 * 5)
            pool.wait_ge(stored_late, 16 * 4)
            pool.wait_ge(state_out, 32 * HEADS)


INPUTS = {}


def _layouts(a):
    f = {k: np.asarray(v) for k, v in a.items()}
    xt = np.concatenate([f["x_prompt"][0], f["x_sample"].reshape(NB * TS, D)], 0).T

    def units(w, cols, kt=8):
        out = []
        for r0, c in cols:
            blk = w[r0:r0 + kt * P, c] if isinstance(c, np.ndarray) else w[r0:r0 + kt * P, c:c + P]
            out.append(blk.reshape(kt, P, P).transpose(1, 0, 2).reshape(P, kt * P))
        return np.stack(out)

    h0 = np.arange(HD)
    pair = [np.concatenate([j * HD + h0, (GRP + j) * HD + h0]) for j in range(GRP)]
    q0 = 3 * A_W
    ab = [(0, q0 + pair[j]) for j in range(GRP)] + [(0, q0 + 512), (0, q0 + 640)]
    for c in range(CA):
        ab += [(0, c * P), (0, 2 * A_W + c * P), (0, A_W + c * P)]
    rows = np.concatenate([np.arange(A_W)] + [A_W + p for p in pair])
    d = {"xT": xt.reshape(KD, P, T).transpose(1, 0, 2),
         "w_in_ab": units(f["w_in_ab"][0], ab),
         "w_out_ab": units(f["w_out_ab"][0][rows], [(0, k * P) for k in range(KD)]),
         "w_in_c": units(f["w_in_c"][0], [(0, o + h * P) for h in range(HEADS) for o in (D, 0, 2 * D, 3 * D)]),
         "w_out_c": units(f["w_out_c"][0], [(0, k * P) for k in range(KD)])}
    for l in range(2):
        d[f"w_up{l}"] = units(f["w_ffn_up"][l], [(0, o + j * P) for j in range(KF) for o in (0, DFF)])
        d[f"w_down{l}"] = units(f["w_ffn_down"][l], [(r * KFH * P, k * P) for k in range(KD) for r in range(2)], KFH)

    def cols(v):
        return v.reshape(-1, P).T

    sinks = f["attn_sinks"][0]
    row = np.arange(P)
    d["vec"] = np.concatenate(
        [cols(f[n][l]) for n in ("norm_mix_pre", "norm_mix_post", "norm_ffn_pre", "norm_ffn_post") for l in range(2)]
        + [cols(f["conv_a_w"][0][t]) for t in range(3)] + [cols(f["ffn_conv_w"][l][t]) for l in range(2) for t in range(3)]
        + [cols(f["hgrn_lb_logits"][l]) for l in range(2)] + [cols(f["hgrn_norm_g"][0])]
        + [np.broadcast_to(sinks, (P, 8)), sinks[4 * (row // 16 % 2) + row // 4 % 4][:, None]], 1)
    d["st_a"] = f["state_conv_a"][0].reshape(NB, 2, CA, P).transpose(3, 2, 0, 1)
    d["st_f"] = f["state_ffn_conv"].reshape(2, NB, 2, KF, P).transpose(4, 0, 3, 1, 2)
    d["kcT"] = f["cache_swa_k"][0].reshape(NB, WIN, P).transpose(2, 0, 1)
    d["vc"] = f["cache_swa_v"][0].reshape(NB, WIN, P)
    d["state0"] = f["state_hgrn"][0].transpose(1, 2, 0, 3)
    return d


_OUTS = {"o_x": (P, KD, T), "o_kp": (P, WIN), "o_ks": (P, NB, WIN), "o_vp": (WIN, P), "o_vs": (NB, WIN, P),
         "o_ca": (P, CA, 2), "o_cs": (P, CA, NB, 2), "o_fp": (P, 2, KF, 2), "o_fs": (P, 2, KF, NB, 2),
         "o_sp": (HEADS, P, P), "o_ss": (HEADS, P, NB, P)}


def kernel(**inputs):
    import concourse.bacc as bacc
    from concourse.bass_utils import run_bass_kernel_spmd

    nc = bacc.Bacc("TRN2", target_bir_lowering=False, num_devices=1)
    arrays, dram = {}, {}
    for name, a in {**_layouts(inputs), **shape_tables()}.items():
        a = np.ascontiguousarray(a)
        arrays["in_" + name] = a
        dram[name] = nc.dram_tensor("in_" + name, a.shape, mybir.dt.from_np(a.dtype), kind="ExternalInput").ap()
    for name, shape in _OUTS.items():
        dram[name] = nc.dram_tensor(name, shape, F32, kind="ExternalOutput").ap()
    build(nc, dram)
    o = run_bass_kernel_spmd(nc, [arrays], core_ids=[0]).results[0]
    o = {n: np.asarray(o[n]).reshape(s) for n, s in _OUTS.items()}

    y = o["o_x"].transpose(2, 1, 0).reshape(T, D)
    kv = (1, WIN, 2, HD)
    return (y[:TP].reshape(1, TP, D), y[TP:].reshape(NB, TS, D),
            o["o_ca"].transpose(2, 1, 0).reshape(1, 1, 2, A_W),
            o["o_cs"].transpose(2, 3, 1, 0).reshape(1, NB, 2, A_W),
            o["o_kp"].T.reshape(1, *kv), o["o_ks"].transpose(1, 2, 0).reshape(1, NB, *kv[1:]),
            o["o_vp"].reshape(1, *kv), o["o_vs"].reshape(1, NB, *kv[1:]),
            o["o_sp"].reshape(1, 1, HEADS, P, P), o["o_ss"].transpose(2, 0, 1, 3).reshape(1, NB, HEADS, P, P),
            o["o_fp"].transpose(1, 3, 2, 0).reshape(2, 1, 2, DFF),
            o["o_fs"].transpose(1, 3, 4, 2, 0).reshape(2, NB, 2, DFF))
```

```python
from contextlib import ExitStack

import numpy as np

import concourse.bass as bass
from concourse import mybir

F32 = mybir.dt.float32
F32R = mybir.dt.float32r
I32 = mybir.dt.int32
ALU = mybir.AluOpType
ACT = mybir.ActivationFunctionType
AX_X = mybir.AxisListType.X

P = 128
D = 1024
TP, NB, TS = 512, 8, 4
T = TP + NB * TS
H = T // 2
KD = D // P
A_W = 512
CA = A_W // P
WIN = 128
NBLK = TP // WIN
HD = 64
GRP = 4
DFF = 2816
KF = DFF // P
KFH = KF // 2
HEADS = 8
CH = 128
NCH = TP // CH
SPANS = (64, 32, 16, 8)
EPS = 1e-6
F_FLOOR = 2e-9
NEG = -1e30

PHASES = [("in_ab", 18, 8), ("out_ab", 8, 8), ("up0", 2 * KF, 8), ("down0", 2 * KD, KFH),
          ("in_c", 4 * HEADS, 8), ("out_c", 8, 8), ("up1", 2 * KF, 8), ("down1", 2 * KD, KFH)]
UNIT0, TILE0, _n, _t = {}, {}, 0, 0
for _name, _units, _kt in PHASES:
    UNIT0[_name], TILE0[_name] = _n, _t
    _n += _units
    _t += _units if _kt == 8 else _units // 2
UNITS = _n
RESCALED = {"in_ab": 0, "up0": 2, "in_c": 4, "up1": 6}

V_GAIN = 0
V_CONVA = V_GAIN + 64
V_CONVF = V_CONVA + 3 * CA
V_LB = V_CONVF + 2 * 3 * KF
V_NG = V_LB + 16
V_SINK = V_NG + 1
V_SINKS = V_SINK + 8
NV = V_SINKS + 1
MIX_PRE, MIX_POST, FFN_PRE, FFN_POST = range(4)


def gain_col(kind, layer):
    return V_GAIN + (kind * 2 + layer) * KD


def half_of(m):
    n, h = divmod(m, 2)
    kt = [k for name, u, k in PHASES if UNIT0[name] <= n < UNIT0[name] + u][0]
    first = (kt + 1) // 2
    return n, h, (0, first)[h], (first, kt - first)[h]


HALF = (KFH + 1) // 2 * P


class Steps:

    def __init__(self, sem):
        self.sem, self.n = sem, 0

    def mark(self, ins):
        ins.then_inc(self.sem, 1)
        self.n = self.n + 1

    def wait(self, eng):
        eng.wait_ge(self.sem, self.n)


def shape_tables():
    slopes = np.exp2(-8.0 * np.arange(1, 9, dtype=np.float32) / 8)
    q, k = np.arange(P)[:, None], np.arange(2 * WIN)[None]
    dist = q + WIN - k
    ok = (dist >= 0) & (dist < WIN)
    bias = np.where(ok[:, None], -slopes[None, :, None] * dist[:, None], NEG).astype(np.float32)
    row = np.arange(P)
    g, j, t = row // 16 % 2, row // 4 % 4, row % 4
    dist = t[:, None] + WIN - np.arange(WIN + TS)[None]
    ok = (dist >= 0) & (dist < WIN)
    bias_s = np.where(ok, -slopes[4 * g + j][:, None] * dist, NEG).astype(np.float32)
    s, t = np.arange(CH)[:, None], np.arange(CH)[None]
    masks = [(s // 8 == t // 8) & (s <= t)]
    for h in SPANS:
        masks.append((s // (2 * h) == t // (2 * h)) & (s % (2 * h) < h) & (t % (2 * h) >= h))
    masks = np.stack(masks, 1).astype(np.int32)
    s, t = np.arange(NB * TS)[:, None], np.arange(NB * TS)[None]
    mask_s = ((s // TS == t // TS) & (s <= t)).astype(np.int32)
    own = (np.arange(3 * NB * TS)[:, None] % (NB * TS) // TS == np.arange(NB)[None]).astype(np.float32)
    own = np.repeat(own[:, :, None], P, 2)
    keep = np.ones((P, T), np.float32)
    keep[:, 0:TP:CH] = 0
    keep[:, TP::TS] = 0
    return {"c_ident": np.eye(P, dtype=np.float32), "c_bias": bias, "c_bias_s": bias_s,
            "c_masks": masks, "c_mask_s": mask_s, "c_own": own, "c_keep": keep}


def build(nc, dram):
    ctx = ExitStack()

    def sb(name, shape, dt=F32, at=ctx):
        return at.enter_context(nc.sbuf_tensor(name, shape, dt))

    def bank(name):
        return ctx.enter_context(nc.psum_tensor(name, [P, 512], F32))

    def sem(name):
        return ctx.enter_context(nc.semaphore(name))

    with ctx:
        x = sb("x", [P, KD, T])
        rstd = sb("rstd", [P, T])
        S = [sb(f"scratch{i}", [P, T]) for i in range(4)]
        vec = sb("vec", [P, NV])
        lb = sb("lb", [P, 8, HEADS])
        eps = sb("eps", [P, 1])
        arrival = sb("arrival", [P, 6])
        ones = sb("ones", [P, P])
        ident = sb("ident", [P, P])
        sp = sb("sp", [P, NB, 2 + TS])
        st_f = sb("st_f", [P, 2, KF, NB, 2])
        tail_f = sb("tail_f", [P, 2, KF, 2])
        st_a = sb("st_a", [P, CA, NB, 2])
        tail_a = sb("tail_a", [P, CA, 2])
        raw = [sb(f"raw{i}", [P, KFH * P]) for i in range(4)]
        w_hi = [sb(f"w_hi{i}", [P, KFH * P], F32R) for i in range(2)]
        w_lo = [sb(f"w_lo{i}", [P, KFH * P], F32R) for i in range(2)]

        with ExitStack() as at:
            h_hi = sb("h_hi", [P, KD, T], F32R, at)
            h_lo = sb("h_lo", [P, KD, T], F32R, at)
        with ExitStack() as at:
            mix = sb("mix", [P, KD, T], F32, at)
            over = sb("mix_rest", [P, KD, T], F32, at)
            with ExitStack() as a:
                y_hi = sb("y_hi", [P, KD, T], F32R, a)
                y_lo = sb("y_lo", [P, KD, T], F32R, a)
                with ExitStack() as b:
                    q_sb = sb("q_sb", [P, GRP, T], F32, b)
                    k_sb = sb("k_sb", [P, T], F32, b)
                    v_sb = sb("v_sb", [P, T], F32, b)
                    kc = sb("kc", [P, NB, WIN + TS], F32, b)
                    vc = sb("vc", [P, NB, P], F32, b)
                    vnew = sb("vnew", [TS, NB, P], F32, b)
                    vtok = sb("vtok", [P, NBLK, P], F32, b)
                    qbd = sb("qbd", [P, NB, 2 * GRP * TS], F32, b)
                    bias = sb("bias", [P, 8, 2 * WIN], F32, b)
                    bias_s = sb("bias_s", [P, WIN + TS], F32, b)
                    pr = [sb(f"pr{i}", [P, GRP, 2 * WIN], F32, b) for i in range(2)]
                    pr_s = sb("pr_s", [P, 2, WIN + TS], F32, b)
                    pT = sb("pT", [P, 2, GRP * P], F32, b)
                    pT_s = sb("pT_s", [P, 2, P], F32, b)
                    pT_n = sb("pT_n", [TS, 2, P], F32, b)
                    sm = sb("sm", [P, 2, 6, GRP], F32, b)
                    sm_s = sb("sm_s", [P, 6, 2], F32, b)
                with ExitStack() as b:
                    kk, G, qn, vv, gn, sg, eG, kd, qG, E1, E2 = [
                        sb(f"c_{n}", [P, T], F32, b)
                        for n in ("kk", "G", "qn", "vv", "gn", "sg", "eG", "kd", "qG", "E1", "E2")]
                    lev = [sb(f"lev{i}", [P, TP], F32, b) for i in range(len(SPANS))]
                    AT = sb("AT", [P, TP], F32, b)
                    AT_s = sb("AT_s", [NB * TS, NB * TS], F32, b)
                    Sst = sb("Sst", [P, NCH, P], F32, b)
                    vt = sb("vt", [P, NCH, P], F32, b)
                    vt_s = sb("vt_s", [NB * TS, P], F32, b)
                    v_hi_s = sb("v_hi_s", [NB * TS, P], F32R, b)
                    kt = sb("kt", [P, NCH, P], F32, b)
                    kt_s = sb("kt_s", [3 * NB * TS, P], F32R, b)
                    v3_s = sb("v3_s", [3 * NB * TS, P], F32, b)
                    S0 = sb("S0", [P, NB, P], F32, b)
                    Snew = sb("Snew", [P, NB, P], F32, b)
                    vbd = sb("vbd", [3 * NB * TS, NB, P], F32R, b)
                    own = sb("own", [3 * NB * TS, NB, P], F32, b)
                    masks = sb("masks", [P, 1 + len(SPANS), CH], I32, b)
                    mask_s = sb("mask_s", [NB * TS, NB * TS], I32, b)
                    keep = sb("keep", [P, T], F32, b)
            with ExitStack() as a:
                g_hi = sb("g_hi", [P, KF, T], F32R, a)
                g_lo = sb("g_lo", [P, KF, T], F32R, a)

        acc = [ctx.enter_context(nc.psum_tensor(f"acc{i}", [P, 2, 512], F32)) for i in range(2)]
        A = [bank(f"aux{i}") for i in range(4)]

        raw_ready = [sem(f"raw_ready{i}") for i in range(4)]
        hi_ready = sem("hi_ready")
        lo_ready = sem("lo_ready")
        half_done = sem("half_done")
        cols_done = sem("cols_done")
        mix_cols = sem("mix_cols")
        sq_cols = sem("sq_cols")
        evac = sem("evac")
        x_in = [sem(f"x_in{k}") for k in range(KD)]
        vec_in = sem("vec_in")
        const_in = sem("const_in")
        const_a = sem("const_a")
        const_c = sem("const_c")
        state0_in = sem("state0_in")
        stored = sem("stored")
        conv_states_out = sem("conv_states_out")
        x_out = sem("x_out")
        state_out = sem("state_out")
        set_up = sem("set_up")
        h_hi_ready = sem("h_hi_ready")
        h_ready = sem("h_ready")
        x_new = sem("x_new")
        sq_ready = sem("sq_ready")
        sq_added = sem("sq_added")
        mix_scaled = sem("mix_scaled")
        stat_done = sem("stat_done")
        rstd_ready = sem("rstd_ready")
        rescaled = sem("rescaled")
        sp_ready = sem("sp_ready")
        tap_ready = sem("tap_ready")
        conv_done = sem("conv_done")
        act_done = sem("act_done")
        gate_ready = sem("gate_ready")
        g_hi_ready = sem("g_hi_ready")
        g_ready = sem("g_ready")
        act_step, dve_step, pool_step = sem("act_step"), sem("dve_step"), sem("pool_step")
        qbd_ready, kc_ready = sem("qbd_ready"), sem("kc_ready")
        vT_done, vT_copied = sem("vT_done"), sem("vT_copied")
        s_done, s_biased, p_exp, p_sum, p_ready = [sem(n) for n in
                                                   ("s_done", "s_biased", "p_exp", "p_sum", "p_ready")]
        pT_done, pT_copied, o_done, yb_hi, yb_lo = [sem(n) for n in
                                                    ("pT_done", "pT_copied", "o_done", "yb_hi", "yb_lo")]
        names = ("fl_ready", "sig_ready", "ff_ready", "lf_ready", "G_ready", "eG_ready", "qG_ready",
                 "kd_diff", "kd_exp", "kd_ready", "lev_diff", "lev_exp", "lev_ready", "diag_diff", "diag_exp",
                 "diag_ready", "al_done", "al_taken", "u_done", "us_done", "st_ready", "oc_done",
                 "osq_ready", "ostat_done", "ors_ready", "og_ready", "oy_ready", "oy_hi", "oy_lo",
                 "kdT_done", "kdT_hi", "kdT_copied", "v_hi", "v_lo", "vcT_done", "vcT_copied", "vbd_ready", "gn_ready",
                 "sg_ready", "gs_ready", "s0_scaled", "snew_ready", "lb_ready", "lb_done")
        C = {n: sem(n) for n in names}

        def tile(name, i):
            return TILE0[name] + i + 1

        def tok2(ap):
            return ap.rearrange("p (a b) -> p a b", a=2)

        def sample(ap, n=TS):
            return ap.rearrange("p (b t) -> p b t", b=NB)

        def later(ap, span):
            return ap.rearrange("p (n a s) -> p n a s", a=2, s=span)[:, :, 1, :]

        R0, R1, R2 = [slice(i * NB * TS, (i + 1) * NB * TS) for i in range(3)]

        def halves_at(t, first):
            return {0: (), 1: (5, 6), 2: ()}.get(t, (t + 4,)) if first else (t + 4,)

        acc_v = [a[:, :, 0:H] for a in acc]
        block = ctx.enter_context(nc.Block())

        @block.sync
        def _(sp_q):
            def unit(name, u, i):
                n, kt_ = UNIT0[name] + u, half_of(2 * UNIT0[name])[3] + half_of(2 * UNIT0[name] + 1)[3]
                if not isinstance(i, int) or n + 4 * i >= 4:
                    sp_q.wait_ge(lo_ready, 2 * (n + 4 * i) - 6)
                src = dram["w_" + name]
                sp_q.dma_start(raw[n % 4][:, 0:kt_ * P], src[u + 4 * i, :, :]
                               ).then_inc(raw_ready[n % 4], 16)

            sp_q.dma_start(vec[:], dram["vec"]).then_inc(vec_in, 16)
            for name, units, kt_ in PHASES:
                if name == "in_ab":
                    for u in range(units):
                        unit(name, u, 0)
                        if u == 1:
                            for k in range(1, KD):
                                sp_q.dma_start(x[:, k, :], dram["xT"][:, k, :]).then_inc(x_in[k], 16)
                        if u == 3:
                            sp_q.dma_start(ident[:], dram["c_ident"]).then_inc(const_in, 16)
                            sp_q.dma_start(st_a[:], dram["st_a"]).then_inc(const_in, 16)
                            sp_q.dma_start(st_f[:], dram["st_f"]).then_inc(const_in, 16)
                        if u == 3:
                            sp_q.dma_start(kc[:, :, 0:WIN], dram["kcT"]).then_inc(const_a, 16)
                            sp_q.dma_start(vc[:], dram["vc"].rearrange("b k f -> k b f")).then_inc(const_a, 16)
                            sp_q.dma_start(bias[:], dram["c_bias"]).then_inc(const_a, 16)
                            sp_q.dma_start(bias_s[:], dram["c_bias_s"]).then_inc(const_a, 16)
                    continue
                with sp_q.Fori(0, units // 4) as i:
                    for u in range(4):
                        unit(name, u, i)
            for k in range(KD):
                sp_q.wait_ge(x_new, 3 * KD + k + 1)
                sp_q.dma_start(dram["o_x"][:, k, :], x[:, k, :]).then_inc(x_out, 16)
            sp_q.wait_ge(x_out, 16 * KD)

        @block.tensor
        def _(pe):
            def half(m, off, out, moving, kt_base, start, stop, tile_waits=None, ks=None, signal=1):
                n, half_, _, kts = half_of(m + off if isinstance(off, int) else m)
                slot = n % 2
                if ks is None or 0 in ks:
                    pe.wait_ge(lo_ready, m + 1 + off)
                for k in ks or range(kts):
                    cols = slice(half_ * HALF + k * P, half_ * HALF + (k + 1) * P)
                    kk_ = kt_base + k
                    if tile_waits is not None:
                        pe.wait_ge(*tile_waits(kk_))
                    passes = [(w_hi, moving[0]), (w_hi, moving[1]), (w_lo, moving[0])]
                    for q, (w, mv) in enumerate(passes):
                        for t in range(2):
                            mm = pe.matmul(acc[out][:, t, 0:H], w[slot][:, cols], mv[:, kk_, t * H:(t + 1) * H],
                                           start=start and k == 0 and q == 0, stop=stop and k == kts - 1 and q == 2)
                if signal:
                    mm.then_inc(half_done, signal)

            def keep_warm(n):
                for _ in range(n):
                    pe.matmul(A[3][:, 0:P], ones[:], ones[:], start=True, stop=True)

            def last_half(m, moving, kt_base):
                n, half_, _, kts = half_of(m)
                pe.wait_ge(lo_ready, m + 1)
                for t in range(2):
                    for k in range(kts):
                        cols = slice(half_ * HALF + k * P, half_ * HALF + (k + 1) * P)
                        for q, (w, mv) in enumerate([(w_hi, moving[0]), (w_hi, moving[1]), (w_lo, moving[0])]):
                            mm = pe.matmul(acc[1][:, t, 0:H], w[n % 2][:, cols],
                                           mv[:, kt_base + k, t * H:(t + 1) * H],
                                           start=False, stop=k == kts - 1 and q == 2)
                    mm.then_inc((cols_done, half_done)[t], 1)

            def first_pair(name, norm):
                m = 2 * UNIT0[name]
                if TILE0[name]:
                    keep_warm(14)
                    pe.wait_ge(evac, TILE0[name])
                for k in range(8):
                    e = k // 4
                    for u in range(2):
                        half(m + 2 * u + e, 0, u, h, 4 * e, e == 0, e == 1, tile_ready(norm // 2) if u == 0 else None,
                             ks=[k % 4], signal={(0, 3): 1, (0, 7): 1, (1, 7): 2}.get((u, k), 0))
                stats(norm)

            def stats(norm):
                for src, ready, count in ((S[2], sq_added, KD - 1), (S[1], sq_ready, KD)):
                    for t in range(2):
                        if src is S[1] and t == 0 and norm % 2:
                            pe.wait_ge(sq_cols, (norm + 1) // 2)
                        else:
                            pe.wait_ge(ready, count * (norm + 1))
                        mm = pe.matmul(A[t][:, 0:H], ones[:], src[:, t * H:(t + 1) * H], start=src is S[2],
                                       stop=src is S[1])
                        if src is S[1]:
                            mm.then_inc(stat_done, 1)

            def tile_ready(norm):
                return lambda k: (h_ready, KD * norm + k + 1)

            h = (h_hi, h_lo)
            def values_transposed(part):
                if part == 0:
                    pe.wait_ge(evac, tile("in_ab", 5))
                    for n in range(NBLK):
                        mm = pe.transpose(A[2][:, n * P:(n + 1) * P], v_sb[:, n * P:(n + 1) * P], ident[:])
                else:
                    b0 = 4 * (part - 1)
                    if part == 2:
                        pe.wait_ge(vT_copied, 1)
                    for b in range(4):
                        c = TP + (b0 + b) * TS
                        mm = pe.transpose(A[4 - part][0:TS, b * P:(b + 1) * P], v_sb[:, c:c + TS], ident[:])
                mm.then_inc(vT_done, 1)

            def sample_scores():
                pe.wait_ge(qbd_ready, 2)
                pe.wait_ge(kc_ready, 1)
                pe.wait_ge(const_a, 64)
                for b in range(NB):
                    r = 32 * (b % 4)
                    mm = pe.matmul(A[b // 4][r:r + 32, 0:WIN + TS], qbd[:, b, :], kc[:, b, :], start=True, stop=True)
                mm.then_inc(s_done, 1)

            def sample_probs_transposed():
                pe.wait_ge(p_ready, 1)
                pe.wait_ge(vT_copied, 3)
                for c in range(2):
                    pe.transpose(A[2][:, c * P:(c + 1) * P], pr_s[:, c, 0:WIN], ident[:])
                    mm = pe.transpose(A[3][0:TS, c * P:(c + 1) * P], pr_s[:, c, WIN:WIN + TS], ident[:])
                mm.then_inc(pT_done, 1)

            def sample_out():
                pe.wait_ge(pT_copied, 2)
                for b in range(NB):
                    r = 32 * (b % 4)
                    pe.matmul(A[2][:, 32 * b:32 * b + 32], vc[:, b, :], pT_s[:, b // 4, r:r + 32], start=True, stop=False)
                    mm = pe.matmul(A[2][:, 32 * b:32 * b + 32], vnew[:, b, :], pT_n[:, b // 4, r:r + 32],
                                   start=False, stop=True)
                mm.then_inc(o_done, 1)

            def scores(s):
                n, g = divmod(s, 2)
                lo_k = WIN if n == 0 else 0
                rows = slice(64 * g, 64 * g + 64)
                pe.wait_ge(s_biased, 2 * s + 2)
                for j in range(GRP):
                    mm = pe.matmul(A[j // 2][:, (j % 2) * 256 + lo_k:(j % 2) * 256 + 256],
                                   q_sb[rows, j, n * WIN:(n + 1) * WIN],
                                   k_sb[rows, (n - 1) * WIN + lo_k:(n + 1) * WIN], start=True, stop=True)
                mm.then_inc(s_done, 1)

            def probs_transposed(s):
                pe.wait_ge(p_ready, s + 2)
                pe.wait_ge(yb_lo, s + 1)
                if s:
                    pe.wait_ge(pT_copied, 2 * s + 2)
                for c in range(1 if s < 2 else 0, 2):
                    for j in range(GRP):
                        mm = pe.transpose(A[2 + c][:, j * P:(j + 1) * P], pr[s % 2][:, j, c * WIN:(c + 1) * WIN], ident[:])
                mm.then_inc(pT_done, 1)

            def attention_out(s):
                n, g = divmod(s, 2)
                pe.wait_ge(pT_copied, 2 * s + 4)
                first = 1 if n == 0 else 0
                for c in range(first, 2):
                    mm = pe.matmul(A[2][64 * g:64 * g + 64, :], vtok[:, n - 1 + c, 64 * g:64 * g + 64], pT[:, c, :],
                                   start=c == first, stop=c == 1)
                mm.then_inc(o_done, 1)

            extra = {12: [lambda: values_transposed(0), lambda: values_transposed(1), sample_scores],
                     13: [lambda: values_transposed(2)],
                     15: [sample_probs_transposed], 16: [sample_out]}
            for s in range(8):
                extra.setdefault(14 + 2 * s, []).append(lambda s=s: scores(s))
                extra.setdefault(17 + 2 * s, []).append(lambda s=s: probs_transposed(s))
                extra.setdefault(18 + 2 * s, []).append(lambda s=s: attention_out(s))
            pe.wait_ge(set_up, 3)
            keep_warm(12)
            first_pair("in_ab", 0)
            pe.wait_ge(const_in, 48)
            for u in range(2, 18):
                pe.wait_ge(evac, u - 1)
                for e in range(2):
                    m = 2 * u + e
                    half(m, 0, u % 2, h, 4 * e, e == 0, e == 1)
                    for f in extra.get(m, []):
                        f()

            def out_phase(name, moving, norm, ready, first=0):
                for tile in range(first, KD):
                    pe.wait_ge(evac, TILE0[name] + tile - 1)
                    for e in range(2):
                        m = 2 * (UNIT0[name] + tile) + e
                        if tile == KD - 1 and e == 1:
                            last_half(m, moving, 4)
                            continue
                        half(m, 0, tile % 2, moving, 4 * e, e == 0, e == 1, ready if tile == 0 else None)
                stats(norm)

            def yb_ready(k):
                return (yb_lo, 9) if k < GRP else (g_ready, k - GRP + 1)

            out_phase("out_ab", (y_hi, y_lo), 1, yb_ready)

            def ffn(layer):
                name = f"up{layer}"
                norm = 2 + 4 * layer

                def up(i, units):
                    for u in units:
                        pe.wait_ge(evac, TILE0[name] + u - 1 + 4 * i)
                        for e in range(2):
                            half(2 * (UNIT0[name] + u) + e, 8 * i, u % 2, h, 4 * e, e == 0, e == 1)

                first_pair(name, norm)
                up(0, (2, 3))
                with pe.Fori(1, KF // 2) as i:
                    up(i, range(4))
                name = f"down{layer}"

                def down(i, peeled_first):
                    for tile in range(2):
                        pe.wait_ge(evac, TILE0[name] + tile - 1 + 2 * i)
                        for r in range(2):
                            if peeled_first and tile == 0:
                                pe.wait_ge(g_ready, CA + KF * layer + (KFH, KF)[r])
                            for e in range(2):
                                if isinstance(i, int) and i == KD // 2 - 1 and (tile, r, e) == (1, 1, 1):
                                    last_half(2 * (UNIT0[name] + 3) + 1 + 8 * i, (g_hi, g_lo), KFH + 6)
                                    continue
                                half(2 * (UNIT0[name] + 2 * tile + r) + e, 8 * i, tile, (g_hi, g_lo),
                                     KFH * r + 6 * e, r == 0 and e == 0, r == 1 and e == 1)

                down(0, True)
                with pe.Fori(1, KD // 2 - 1) as i:
                    down(i, False)
                down(KD // 2 - 1, False)
                stats(norm + 1)

            ffn(0)

            def levels(hd, which):
                b = (1, 2, 3, 0, 1)[which]
                lhs, rhs = (E2, E1) if which == 0 else (lev[which - 1], lev[which - 1])
                for c in range(NCH):
                    cs = slice(c * CH, (c + 1) * CH)
                    out, moving = A[b][:, cs], rhs[:, cs]
                    if which:
                        out = A[b][:, c * (CH // 2):(c + 1) * (CH // 2)]
                        moving = later(moving, SPANS[which - 1])
                    mm = pe.matmul(out, lhs[:, cs], moving, start=True, stop=True)
                mm.then_inc(C["al_done"], 1)

            def hgrn_tick(t, prev, cur):
                if prev is not None:
                    if t == 0:
                        pe.wait_ge(C["diag_ready"], 2 * prev + 2)
                        pe.wait_ge(C["v_hi"], prev + 1)
                        levels(prev, 0)
                        pe.wait_ge(C["st_ready"], prev + 1)
                        pe.matmul(A[2][0:NB * TS, 0:NB * TS], E2[:, TP:T], E1[:, TP:T], start=True, stop=True
                                  ).then_inc(C["al_done"], 1)
                    if t == 1:
                        pe.wait_ge(C["lev_ready"], 8 * prev + 8)
                        pe.wait_ge(C["al_taken"], 6 * prev + 2)
                        levels(prev, 1)
                        levels(prev, 2)
                    if t == 2:
                        levels(prev, 3)
                        levels(prev, 4)
                    if t == 3:
                        pe.wait_ge(C["al_taken"], 6 * prev + 6)
                        pe.wait_ge(C["vbd_ready"], prev + 1)
                        for z in range(2):
                            pe.matmul(A[z][:, :], kt_s[:], vbd[:, 4 * z:4 * z + 4, :], start=True, stop=True
                                      ).then_inc(C["us_done"], 1)
                        pe.wait_ge(C["qG_ready"], prev + 1)
                        pe.wait_ge(state0_in, 16 * prev + 16)
                        for c in range(NCH):
                            cs = slice(c * CH, (c + 1) * CH)
                            mm = pe.matmul(A[3][:, cs], vt[:, c, :], AT[:, cs], start=True, stop=c == 0)
                            if c:
                                mm = pe.matmul(A[3][:, cs], Sst[:, c - 1, :], qG[:, cs], start=False, stop=True)
                        pe.matmul(A[2][:, 0:NB * TS], vt_s[:], AT_s[:], start=True, stop=False,
                                  skip_group_check=True)
                        for b in range(NB):
                            mm = pe.matmul(A[2][:, b * TS:(b + 1) * TS], S0[:, b, :], qG[:, TP + b * TS:TP + (b + 1) * TS],
                                           start=False, stop=True, skip_group_check=True)
                        mm.then_inc(C["oc_done"], 1)
                    if t == 4:
                        pe.wait_ge(C["snew_ready"], 2 * prev + 2)
                        pe.wait_ge(C["osq_ready"], prev + 1)
                        pe.matmul(A[0][:, 0:H], ones[:], S[2][:, 0:H], start=True, stop=True)
                        pe.matmul(A[1][:, 0:H], ones[:], S[2][:, H:T], start=True, stop=True
                                  ).then_inc(C["ostat_done"], 1)
                if cur is not None:
                    if t == (6 if prev is None else 5):
                        if prev is None:
                            keep_warm(20)
                        pe.wait_ge(C["kd_ready"], cur + 1)
                        if prev is not None:
                            pe.wait_ge(C["ors_ready"], prev + 1)
                        for c in range(NCH):
                            pe.transpose(A[0][:, c * P:(c + 1) * P], kd[:, c * CH:(c + 1) * CH], ident[:])
                        pe.transpose(A[1][0:NB * TS, 0:P], kd[:, TP:T], ident[:]).then_inc(C["kdT_done"], 1)
                    if t == 6:
                        pe.wait_ge(evac, tile("in_c", 2) + 4 * cur)
                        pe.wait_ge(C["kdT_copied"], cur + 1)
                        for c in range(NCH):
                            pe.transpose(A[0][:, c * P:(c + 1) * P], vv[:, c * CH:(c + 1) * CH], ident[:])
                        pe.transpose(A[1][0:NB * TS, 0:P], vv[:, TP:T], ident[:]).then_inc(C["vcT_done"], 1)
                    if t == 7:
                        pe.wait_ge(C["vcT_copied"], cur + 1)
                        if prev is not None:
                            pe.wait_ge(C["og_ready"], prev + 1)
                        for c in range(NCH):
                            mm = pe.matmul(A[2][:, c * P:(c + 1) * P], kt[:, c, :], vt[:, c, :], start=True, stop=True)
                        mm.then_inc(C["u_done"], 1)

            def head(hd, prev, units):
                for u in units:
                    pe.wait_ge(evac, TILE0["in_c"] + u - 1 + 4 * hd)
                    for e in range(2):
                        half(2 * (UNIT0["in_c"] + u) + e, 8 * hd, u % 2, h, 4 * e, e == 0, e == 1)
                        hgrn_tick(2 * u + e, prev, hd)

            first_pair("in_c", 4)
            head(0, None, (2, 3))
            with pe.Fori(1, HEADS) as hd:
                head(hd, hd - 1, range(4))

            def yc_ready(k):
                return (C["oy_lo"], k + 1)

            m = 2 * UNIT0["out_c"]
            for u in range(2):
                pe.wait_ge(evac, TILE0["out_c"] + u - 1)
                for e in range(2):
                    for t in ((0,), (1, 2), (3,), (4,))[2 * u + e]:
                        hgrn_tick(t, HEADS - 1, None)
                    half(m + 2 * u + e, 0, u, (y_hi, y_lo), 4 * e, e == 0, False, yc_ready if u == 0 else None,
                         ks=range(4 - e), signal=int(m + 2 * u + e == m))
            for u in range(2):
                half(m + 2 * u + 1, 0, u, (y_hi, y_lo), 4, False, True, yc_ready if u == 0 else None,
                     ks=[3], signal=1 + u)
            out_phase("out_c", (y_hi, y_lo), 5, None, first=2)
            ffn(1)

        @block.scalar
        def _(act):
            step = Steps(act_step)

            def split(m, off):
                s = m + off if isinstance(off, int) else m
                if s >= 2 * UNITS:
                    return
                n, h_, kt0, kts = half_of(s)
                if h_ == 0:
                    act.wait_ge(raw_ready[n % 4], 16 * ((m // 2) // 4 + 1) + (off * 2))
                if not isinstance(off, int) or s >= 4:
                    act.wait_ge(half_done, m - 3 + off)
                cols = slice(kt0 * P, (kt0 + kts) * P)
                act.copy(w_hi[n % 2][:, h_ * HALF:h_ * HALF + kts * P], raw[n % 4][:, cols]).then_inc(hi_ready, 1)

            def buffer_free(norm, k):
                if not isinstance(k, int) or (KD - 1) * norm + k >= 2:
                    act.wait_ge(sq_added, (KD - 1) * norm - 1 + k)

            def norm_root(norm, out):
                for t in range(2):
                    cols = slice(t * H, (t + 1) * H)
                    act.wait_ge(stat_done, 2 * norm + t + 1)
                    step.mark(act.activation(out[:, cols], A[t][:, 0:H], ACT.Ln, bias=eps[:], scale=1.0 / D))
                    step.wait(act)
                    act.activation(out[:, cols], out[:, cols], ACT.Exp, scale=-0.5).then_inc(rstd_ready, 1)

            def normed(pre, col, name, arrived):
                for k in range(KD):
                    arrived(k)
                    act.activation(h_hi[:, k, :], x[:, k, :], ACT.Copy, scale=vec[:, k + col:k + col + 1]
                                   ).then_inc(h_hi_ready, 1)
                    if name == "in_ab" and k < 2:
                        split(2 * k, 0)
                        split(2 * k + 1, 0)
                    if k == (7 if name == "in_ab" else 6):
                        split(2 * UNIT0[name] + 4, 0)
                    buffer_free(2 * pre, k)
                    act.activation(S[k % 2][:], x[:, k, :], ACT.Square).then_inc(sq_ready, 1)

            act.dma_start(x[:, 0, :], dram["xT"][:, 0, :]).then_inc(x_in[0], 16)
            act.preload_act_table_set("natural_log_exp_and_others")
            act.wait_ge(set_up, 3)
            act.wait_ge(vec_in, 16)
            normed(0, gain_col(MIX_PRE, 0), "in_ab", lambda k: act.wait_ge(x_in[k], 16))

            def exps(s):
                act.wait_ge(p_sum, 2 * s + 3)
                if s < 0:
                    for c in range(2):
                        act.activation(pr_s[:, c, :], pr_s[:, c, :], ACT.Exp, bias=sm_s[:, 0, c:c + 1],
                                       accum_out=sm_s[:, 1, c:c + 1])
                    act.activation(sm_s[:, 3, :], sm_s[:, 2, :], ACT.Exp).then_inc(p_exp, 1)
                    return
                w = slice(WIN, 2 * WIN) if s < 2 else slice(0, 2 * WIN)
                z = sm[:, s % 2]
                for j in range(GRP):
                    act.activation(pr[s % 2][:, j, w], pr[s % 2][:, j, w], ACT.Exp, bias=z[:, 0, j:j + 1],
                                   accum_out=z[:, 1, j:j + 1])
                act.activation(z[:, 3, :], z[:, 2, :], ACT.Exp).then_inc(p_exp, 1)

            def probs_copied(s):
                act.wait_ge(pT_done, s + 2)
                if s < 0:
                    act.copy(pT_s[:].rearrange("p a b -> p (a b)"), A[2][:, 0:2 * P]).then_inc(pT_copied, 1)
                    act.copy(pT_n[:].rearrange("p a b -> p (a b)"), A[3][0:TS, 0:2 * P]).then_inc(pT_copied, 1)
                    return
                if s:
                    act.wait_ge(o_done, s + 1)
                if s < 2:
                    act.copy(pT[:, 1, :], A[3][:]).then_inc(pT_copied, 2)
                    return
                for c in range(2):
                    act.copy(pT[:, c, :], A[2 + c][:]).then_inc(pT_copied, 1)

            def attention_hi(s):
                act.wait_ge(o_done, s + 2)
                if s < 0:
                    for g in range(2):
                        r = slice(64 * g, 64 * g + 64)
                        src = A[2][r, 0:256].rearrange("p (b c) -> p b c", b=NB)[:, :, 16 * g:16 * g + 16]
                        dst = y_hi[r, 0:GRP, TP:T].rearrange("p j (b t) -> p b j t", b=NB)
                        i_ = act.copy(dst, src.rearrange("p b (j t) -> p b j t", j=GRP))
                    i_.then_inc(yb_hi, 1)
                    return
                n, g = divmod(s, 2)
                r = slice(64 * g, 64 * g + 64)
                act.copy(y_hi[r, 0:GRP, n * WIN:(n + 1) * WIN], A[2][r, :].rearrange("p (j q) -> p j q", j=GRP)
                         ).then_inc(yb_hi, 1)

            extra = {12: [lambda: vT(0), lambda: vT(1)], 13: [lambda: vT(2), lambda: exps(-1)],
                     15: [lambda: probs_copied(-1)], 16: [lambda: attention_hi(-1)]}
            for s in range(8):
                extra.setdefault(15 + 2 * s, []).append(lambda s=s: exps(s))
                extra.setdefault(17 + 2 * s, []).append(lambda s=s: probs_copied(s))
                extra.setdefault(18 + 2 * s, []).append(lambda s=s: attention_hi(s))

            def vT(part):
                act.wait_ge(vT_done, part + 1)
                if part == 0:
                    act.copy(vtok[:].rearrange("p a b -> p (a b)"), A[2][:]).then_inc(vT_copied, 1)
                else:
                    b = slice(4 * part - 4, 4 * part)
                    act.copy(vnew[:, b, :].rearrange("p a b -> p (a b)"), A[4 - part][0:TS, :]).then_inc(vT_copied, 1)

            for m in range(1, 36):
                if m == 1:
                    split(5, 0)
                    split(6, 0)
                    norm_root(0, rstd)
                elif m > 2:
                    split(m + 4, 0)
                c, r = divmod(m - 12, 6)
                if m >= 12 and r == 3:
                    act.wait_ge(evac, tile("in_ab", 7 + 3 * c))
                    act.activation(S[1][:], S[3][:], ACT.Copy, scale=vec[:, V_CONVA + 2 * CA + c:V_CONVA + 2 * CA + c + 1]
                                   ).then_inc(tap_ready, 1)
                if m >= 12 and r == 5:
                    act.wait_ge(evac, tile("in_ab", 8 + 3 * c))
                    act.copy(y_hi[:, GRP + c, :], S[0][:]).then_inc(g_hi_ready, 1)
                for f in extra.get(m, []):
                    f()
                if m == 13:
                    act.wait_ge(evac, tile("in_ab", 4))
                    act.dma_start(dram["o_kp"], k_sb[:, TP - WIN:TP]).then_inc(stored, 16)
                    act.wait_ge(kc_ready, 1)
                    act.wait_ge(const_a, 64)
                    act.dma_start(dram["o_ks"], kc[:, :, TS:TS + WIN]).then_inc(stored, 16)
                    act.wait_ge(vT_copied, 3)
                    act.dma_start(dram["o_vp"], vtok[:, NBLK - 1, :]).then_inc(stored, 16)
                    act.dma_start(dram["o_vs"][:, 0:WIN - TS, :].rearrange("b k f -> k b f"), vc[TS:WIN, :, :]
                                  ).then_inc(stored, 16)
                    act.dma_start(dram["o_vs"][:, WIN - TS:WIN, :].rearrange("b k f -> k b f"), vnew[:]
                                  ).then_inc(stored, 16)

            def out_tile(count, norm, k, e):
                buffer_free(norm, k)
                act.wait_ge(evac, count)
                act.activation(S[e][:], mix[:, k, :], ACT.Square).then_inc(sq_ready, 1)

            def last_out(norm):
                k = KD - 1
                buffer_free(norm, k)
                act.wait_ge(mix_cols, (norm + 1) // 2)
                act.activation(S[1][:, 0:H], mix[:, k, 0:H], ACT.Square).then_inc(sq_cols, 1)
                act.wait_ge(evac, TILE0[("out_ab", "down0", "out_c", "down1")[norm // 2]] + KD)
                act.activation(S[1][:, H:T], mix[:, k, H:T], ACT.Square).then_inc(sq_ready, 1)

            def out_phase(name, norm):
                for k in range(KD):
                    split(2 * (UNIT0[name] + k) + 4, 0)
                    if k == KD - 1:
                        last_out(norm)
                    split(2 * (UNIT0[name] + k) + 5, 0)
                    if k < KD - 1:
                        out_tile(tile(name, k), norm, k, k % 2)

            def boundary(post, pre_kind=None, layer=None, name=None):
                norm_root(post, S[3])
                if post == 3:
                    for to, table in ((masks, "c_masks"), (mask_s, "c_mask_s"), (own, "c_own"), (keep, "c_keep")):
                        act.dma_start(to[:], dram[table]).then_inc(const_c, 16)
                    act.dma_start(S0[:], dram["state0"][0, :, :, :]).then_inc(state0_in, 16)
                pre = (post + 1) // 2
                if pre == 4:
                    return
                normed(pre, gain_col(pre_kind, layer), name, lambda k: act.wait_ge(x_new, KD * (pre - 1) + 1 + k))

            out_phase("out_ab", 1)
            boundary(1, FFN_PRE, 0, "up0")
            act.wait_ge(stored, 5 * 16)

            def ffn(layer):
                name = f"up{layer}"

                def up(i, s_off, first=False):
                    for u in range(2):
                        pair = CA + KF * layer + u + 2 * i
                        for t in range(4):
                            for q in halves_at(t, first and u == 0):
                                split(2 * UNIT0[name] + 4 * u + q + s_off, 8 * i if s_off == 0 else 0)
                            if t == 1 and u == 0 and first:
                                norm_root(2 + 4 * layer, rstd)
                            if t == 1:
                                if first and u == 0:
                                    act.wait_ge(rescaled, RESCALED[name] + 1)
                                else:
                                    act.wait_ge(evac, tile(name, 2 * u) + 4 * i)
                                w = V_CONVF + (layer * 3 + 2) * KF
                                act.activation(S[1][:], S[0][:], ACT.Copy, scale=vec[:, bass.ds(w + u + 2 * i, 1)]
                                               ).then_inc(tap_ready, 1)
                            if t == 2:
                                act.wait_ge(conv_done, pair + 1)
                                act.activation(S[2][:], S[1][:], ACT.Gelu_apprx_tanh).then_inc(act_done, 1)
                            if t == 3:
                                if first and u == 0:
                                    act.wait_ge(rescaled, RESCALED[name] + 2)
                                else:
                                    act.wait_ge(evac, tile(name, 2 * u + 1) + 4 * i)
                                act.copy(g_hi[:, u + 2 * i, :], S[3][:]).then_inc(g_hi_ready, 1)

                up(0, 0, True)
                act.preload_act_table_set("gelu_apprx_tanh_and_others")
                with act.Fori(1, KF // 2 - 1) as i:
                    up(i, 0)
                up(KF // 2 - 1, 8 * (KF // 2 - 1))
                name = f"down{layer}"

                def down(i, s_off):
                    for e in range(2):
                        last = e == 1 and s_off > 0
                        for t in range(4):
                            if last and t == 3:
                                last_out(3 + 4 * layer)
                            split(2 * UNIT0[name] + 4 * e + t + 4 + s_off, 8 * i if s_off == 0 else 0)
                        if not last:
                            out_tile(tile(name, e) + 2 * i, 3 + 4 * layer, 2 * i + e, e)

                with act.Fori(0, KD // 2 - 1) as i:
                    down(i, 0)
                act.preload_act_table_set("natural_log_exp_and_others")
                down(KD // 2 - 1, 8 * (KD // 2 - 1))
                if layer == 0:
                    boundary(3, MIX_PRE, 1, "in_c")
                else:
                    boundary(7)

            ffn(0)

            act.wait_ge(C["lb_ready"], 1)
            act.activation(lb[:, 1:3, :], lb[:, 1:3, :], ACT.Exp).then_inc(C["lb_done"], 1)

            STEPS_C = 7

            def hgrn_tick(t, prev, cur):
                if prev is not None:
                    if t == 0:
                        act.wait_ge(C["gn_ready"], prev + 1)
                        step.mark(act.activation(sg[:], sg[:], ACT.Exp, scale=-1.0))
                        step.wait(act)
                        step.mark(act.activation(sg[:], sg[:], ACT.Ln, bias=1.0))
                        step.wait(act)
                        act.activation(sg[:], sg[:], ACT.Exp, scale=-1.0).then_inc(C["sg_ready"], 1)
                    if t == 3:
                        act.wait_ge(C["oc_done"], prev + 1)
                        act.activation(S[2][:, 0:TP], A[3][:], ACT.Square)
                        act.activation(S[2][:, TP:T], A[2][:, 0:NB * TS], ACT.Square).then_inc(C["osq_ready"], 1)
                        if cur is not None:
                            act.wait_ge(C["s0_scaled"], prev + 1)
                            act.dma_start(S0[:], dram["state0"][cur, :, :, :]).then_inc(state0_in, 16)
                    if t == 4:
                        act.wait_ge(C["ostat_done"], prev + 1)
                        for z in range(2):
                            step.mark(act.activation(S[3][:, z * H:(z + 1) * H], A[z][:, 0:H], ACT.Ln, bias=eps[:],
                                                       scale=1.0 / P))
                        step.wait(act)
                        act.activation(S[3][:], S[3][:], ACT.Exp, scale=-0.5).then_inc(C["ors_ready"], 1)
                        act.wait_ge(C["snew_ready"], 2 * prev + 2)
                        act.dma_start(dram["o_ss"][prev, :, :, :], Snew[:]).then_inc(state_out, 16)
                        act.dma_start(dram["o_sp"][prev, :, :], Sst[:, NCH - 1, :]).then_inc(state_out, 16)
                if cur is not None:
                    if t == 1:
                        act.wait_ge(C["fl_ready"], cur + 1)
                        step.mark(act.activation(S[0][:], S[0][:], ACT.Exp, scale=-1.0))
                        step.wait(act)
                        step.mark(act.activation(S[1][:], S[0][:], ACT.Ln, bias=1.0))
                        step.wait(act)
                        act.activation(S[1][:], S[1][:], ACT.Exp, scale=-1.0).then_inc(C["sig_ready"], 1)
                    if t == 2:
                        act.wait_ge(C["ff_ready"], cur + 1)
                        act.activation(S[1][:], S[1][:], ACT.Ln).then_inc(C["lf_ready"], 1)
                    if t == 3:
                        act.wait_ge(C["G_ready"], cur + 1)
                        act.activation(eG[:], G[:], ACT.Exp).then_inc(C["eG_ready"], 1)
                        act.wait_ge(C["kd_diff"], cur + 1)
                        act.activation(kd[:], kd[:], ACT.Exp).then_inc(C["kd_exp"], 1)
                    if t == 5:
                        act.wait_ge(C["kdT_done"], cur + 1)
                        act.copy(kt[:].rearrange("p a b -> p (a b)"), A[0][:])
                        act.copy(kt_s[R1, :], A[1][R0, 0:P])
                        act.copy(kt_s[R0, :], A[1][R0, 0:P]).then_inc(C["kdT_hi"], 1)
                if prev is not None and t == 5:
                    act.wait_ge(C["oy_ready"], prev + 1)
                    act.copy(y_hi[:, prev, :], S[3][:]).then_inc(C["oy_hi"], 1)
                if cur is not None:
                    if 4 <= t <= 7:
                        l = t - 4
                        act.wait_ge(C["lev_diff"], 4 * cur + l + 1)
                        v = lev[l][:].rearrange("p (n a s) -> p n a s", a=2, s=SPANS[l])
                        act.activation(v[:, :, 0, :], v[:, :, 0, :], ACT.Exp, scale=-1.0)
                        act.activation(v[:, :, 1, :], v[:, :, 1, :], ACT.Exp).then_inc(C["lev_exp"], 1)
                    if t == 6:
                        act.wait_ge(C["diag_diff"], cur + 1)
                        act.activation(E1[:], E2[:], ACT.Exp)
                        act.activation(E2[:], E2[:], ACT.Exp, scale=-1.0).then_inc(C["diag_exp"], 1)
                        act.wait_ge(C["vcT_done"], cur + 1)
                        act.copy(vt[:].rearrange("p a b -> p (a b)"), A[0][:])
                        act.copy(vt_s[:], A[1][R0, 0:P]).then_inc(C["vcT_copied"], 1)
                        step.mark(act.copy(v_hi_s[:], A[1][R0, 0:P]))
                        step.wait(act)
                        act.copy(v3_s[R2, :], v_hi_s[:])
                        act.copy(v3_s[R0, :], v_hi_s[:]).then_inc(C["v_hi"], 1)

            def head(hd, prev, s_off):
                for t in range(8):
                    for q in halves_at(t, prev is None):
                        split(2 * UNIT0["in_c"] + q + s_off, 8 * hd if s_off == 0 else 0)
                    if isinstance(hd, int) and hd == 0 and t == 1:
                        norm_root(4, rstd)
                    hgrn_tick(t, prev, hd)

            head(0, None, 0)
            base = step.n
            with act.Fori(1, HEADS - 1) as hd:
                step.n = base + STEPS_C * (hd - 1)
                head(hd, hd - 1, 0)
            step.n = base + STEPS_C * (HEADS - 2)
            head(HEADS - 1, HEADS - 2, 8 * (HEADS - 1))
            assert step.n == base + STEPS_C * (HEADS - 1), step.n - base
            for t in range(6):
                hgrn_tick(t, HEADS - 1, None)
            out_phase("out_c", 5)
            boundary(5, FFN_PRE, 1, "up1")
            act.wait_ge(state_out, 32 * HEADS)
            ffn(1)

        @block.vector
        def _(dve):
            step = Steps(dve_step)

            def split(m, off):
                s = m + off if isinstance(off, int) else m
                if s >= 2 * UNITS:
                    return
                n, h_, kt0, kts = half_of(s)
                dve.wait_ge(hi_ready, m + 1 + off)
                cols, to = slice(kt0 * P, (kt0 + kts) * P), slice(h_ * HALF, h_ * HALF + kts * P)
                dve.tensor_tensor(w_lo[n % 2][:, to], raw[n % 4][:, cols], w_hi[n % 2][:, to], ALU.subtract
                                  ).then_inc(lo_ready, 1)

            def col(c, k):
                return vec[:, c + k:c + k + 1] if isinstance(k, int) else vec[:, bass.ds(k + c, 1)]

            def h_lo_tile(pre, k, c):
                dve.wait_ge(h_hi_ready, KD * pre + 1 + k)
                dve.scalar_tensor_tensor(h_lo[:, k, :], x[:, k, :], col(c, k), h_hi[:, k, :], ALU.mult, ALU.subtract
                                         ).then_inc(h_ready, 1)

            def conv(src, w0, w1, count, sample_count):
                dve.wait_ge(tap_ready, count + 1)
                dve.wait_ge(sp_ready, sample_count + 1)
                y = S[1]
                ys = sample(y[:, TP:T])
                step.mark(dve.scalar_tensor_tensor(y[:, 1:TP], src[:, 0:TP - 1], w1, y[:, 1:TP], ALU.mult, ALU.add))
                step.mark(dve.scalar_tensor_tensor(ys, sp[:, :, 1:1 + TS], w1, ys, ALU.mult, ALU.add))
                step.wait(dve)
                dve.scalar_tensor_tensor(y[:, 2:TP], src[:, 0:TP - 2], w0, y[:, 2:TP], ALU.mult, ALU.add)
                dve.scalar_tensor_tensor(ys, sp[:, :, 0:TS], w0, ys, ALU.mult, ALU.add).then_inc(conv_done, 1)

            dve.wait_ge(vec_in, 16)
            for k in range(KD):
                h_lo_tile(0, k, gain_col(MIX_PRE, 0))
                if k < 2:
                    split(2 * k, 0)
                    split(2 * k + 1, 0)
            split(4, 0)

            def first_pair(name, outs):
                m = 2 * UNIT0[name]
                for u, out in enumerate(outs):
                    dve.wait_ge(half_done, m + 2 * u + 2)
                    dve.tensor_copy(tok2(out), acc_v[u]).then_inc(evac, 1)
                for q in halves_at(1, True):
                    split(m + q, 0)
                dve.wait_ge(evac, TILE0[name] + 2)

            def lower_bounds_a():
                l0, l1 = [vec[:, V_LB + HEADS * i:V_LB + HEADS * (i + 1)] for i in range(2)]
                step.mark(dve.tensor_tensor(lb[:, 0, :], l0, l1, ALU.max))
                step.wait(dve)
                dve.tensor_tensor(lb[:, 1, :], l0, lb[:, 0, :], ALU.subtract)
                dve.tensor_tensor(lb[:, 2, :], l1, lb[:, 0, :], ALU.subtract).then_inc(C["lb_ready"], 1)

            def lower_bounds_b():
                dve.wait_ge(C["lb_done"], 1)
                step.mark(dve.tensor_tensor(lb[:, 3, :], lb[:, 1, :], lb[:, 2, :], ALU.add))
                step.wait(dve)
                step.mark(dve.reciprocal(lb[:, 4, :], lb[:, 3, :]))
                step.wait(dve)
                dve.tensor_tensor(lb[:, 5, :], lb[:, 1, :], lb[:, 4, :], ALU.mult)
                step.mark(dve.tensor_tensor(lb[:, 6, :], lb[:, 2, :], lb[:, 4, :], ALU.mult))
                step.wait(dve)
                step.mark(dve.tensor_tensor(lb[:, 6, :], lb[:, 5, :], lb[:, 6, :], ALU.add))
                step.wait(dve)
                step.mark(dve.tensor_tensor(lb[:, 6, :], lb[:, 6, :], lb[:, 5, :], ALU.subtract))
                step.wait(dve)
                step.mark(dve.tensor_scalar(lb[:, 6, :], lb[:, 6, :], 0.0, 1.0, ALU.max, ALU.min))
                step.wait(dve)
                step.mark(dve.tensor_scalar(lb[:, 7, :], lb[:, 6, :], -1.0, 1.0, ALU.mult, ALU.add))

            def softmax_in(s):
                dve.wait_ge(s_done, s + 2)
                dve.wait_ge(const_a, 64)
                if s < 0:
                    for c in range(2):
                        dve.tensor_tensor(pr_s[:, c, :], A[c][:, 0:WIN + TS], bias_s[:], ALU.add).then_inc(s_biased, 1)
                    view, sink = pr_s[:], vec[:, V_SINKS:V_SINKS + 1].broadcast_to([P, 2])
                    z = sm_s
                else:
                    g = s % 2
                    w = slice(WIN, 2 * WIN) if s < 2 else slice(0, 2 * WIN)
                    if s >= 2:
                        dve.wait_ge(pT_done, s)
                    for a in range(2):
                        dve.tensor_tensor(pr[g][:, 2 * a:2 * a + 2, w],
                                          A[a][:].rearrange("p (j k) -> p j k", j=2)[:, :, w],
                                          bias[:, 4 * g + 2 * a:4 * g + 2 * a + 2, w], ALU.add).then_inc(s_biased, 1)
                    view, sink = pr[g][:, :, w], vec[:, V_SINK + 4 * g:V_SINK + 4 * g + 4]
                    z = sm[:, g]
                dve.wait_ge(s_biased, 2 * s + 4)
                step.mark(dve.tensor_reduce(z[:, 4, :], view, AX_X, ALU.max))
                step.wait(dve)
                step.mark(dve.tensor_tensor(z[:, 5, :], z[:, 4, :], sink, ALU.max))
                step.wait(dve)
                dve.tensor_scalar(z[:, 0, :], z[:, 5, :], -1.0, None, ALU.mult)
                dve.tensor_tensor(z[:, 2, :], sink, z[:, 5, :], ALU.subtract).then_inc(p_sum, 1)

            def softmax_sum(s):
                z = sm_s if s < 0 else sm[:, s % 2]
                dve.wait_ge(p_exp, s + 2)
                step.mark(dve.tensor_tensor(z[:, 4, :], z[:, 1, :], z[:, 3, :], ALU.add))
                step.wait(dve)
                dve.reciprocal(z[:, 5, :], z[:, 4, :]).then_inc(p_sum, 1)

            def attention_lo(s):
                dve.wait_ge(yb_hi, s + 2)
                if s < 0:
                    for g in range(2):
                        r = slice(64 * g, 64 * g + 64)
                        src = A[2][r, 0:256].rearrange("p (b c) -> p b c", b=NB)[:, :, 16 * g:16 * g + 16]
                        src = src.rearrange("p b (j t) -> p b j t", j=GRP)
                        hi, lo = [y[r, 0:GRP, TP:T].rearrange("p j (b t) -> p b j t", b=NB) for y in (y_hi, y_lo)]
                        i_ = dve.tensor_tensor(lo, src, hi, ALU.subtract)
                    i_.then_inc(yb_lo, 1)
                    return
                n, g = divmod(s, 2)
                r, c = slice(64 * g, 64 * g + 64), slice(n * WIN, (n + 1) * WIN)
                dve.tensor_tensor(y_lo[r, 0:GRP, c], A[2][r, :].rearrange("p (j q) -> p j q", j=GRP),
                                  y_hi[r, 0:GRP, c], ALU.subtract).then_inc(yb_lo, 1)

            extra = {12: [lambda: softmax_in(-1)], 13: [lambda: softmax_sum(-1)], 16: [lambda: attention_lo(-1)]}
            for s in range(8):
                extra.setdefault(14 + 2 * s, []).append(lambda s=s: softmax_in(s))
                extra.setdefault(15 + 2 * s, []).append(lambda s=s: softmax_sum(s))
                extra.setdefault(18 + 2 * s, []).append(lambda s=s: attention_lo(s))

            lower_bounds_a()
            first_pair("in_ab", (q_sb[:, 0, :], q_sb[:, 1, :]))
            dve.wait_ge(rstd_ready, 2)
            for u in range(2):
                dve.scalar_tensor_tensor(q_sb[:, u, :], q_sb[:, u, :], HD ** -0.5, rstd[:], ALU.mult, ALU.mult
                                         ).then_inc(rescaled, 1)
            for m in range(3, 36):
                u = m // 2
                if m % 2 and m > 3:
                    dve.wait_ge(half_done, m + 1)
                    src, r2 = acc_v[u % 2], tok2(rstd[:])
                    c, r = divmod(u - 6, 3)
                    if u < 4:
                        dve.scalar_tensor_tensor(tok2(q_sb[:, u, :]), src, HD ** -0.5, r2, ALU.mult, ALU.mult
                                                 ).then_inc(evac, 1)
                    elif u < 6:
                        dve.tensor_tensor(tok2((k_sb, v_sb)[u - 4][:]), src, r2, ALU.mult).then_inc(evac, 1)
                    elif r == 0:
                        if c:
                            dve.wait_ge(g_ready, c)
                        dve.tensor_tensor(tok2(S[0][:]), src, r2, ALU.mult).then_inc(evac, 1)
                    elif r == 1:
                        dve.wait_ge(gate_ready, 2 * c + 1)
                        dve.tensor_tensor(tok2(S[3][:]), src, tok2(S[0][:]), ALU.mult).then_inc(evac, 1)
                    else:
                        dve.wait_ge(gate_ready, 2 * c + 2)
                        dve.tensor_tensor(tok2(S[0][:]), src, tok2(S[1][:]), ALU.mult).then_inc(evac, 1)
                split(m + 4, 0)
                if m >= 12 and (m - 12) % 6 == 4:
                    c = (m - 12) // 6
                    conv(S[3], col(V_CONVA, c), col(V_CONVA + CA, c), c, c)
                for f in extra.get(m, []):
                    f()
                if m >= 12 and (m - 12) % 6 == 5:
                    c = (m - 12) // 6
                    dve.wait_ge(g_hi_ready, c + 1)
                    dve.tensor_tensor(y_lo[:, GRP + c, :], S[0][:], y_hi[:, GRP + c, :], ALU.subtract).then_inc(g_ready, 1)

            def out_tile(u_done, out, k):
                dve.wait_ge(half_done, u_done)
                dve.tensor_copy(tok2(mix[:, k, :]), acc_v[out]).then_inc(evac, 1)

            def last_out(u_done, post):
                for t, (done, count, out) in enumerate(((cols_done, post, mix_cols), (half_done, u_done, evac))):
                    dve.wait_ge(done, count)
                    dve.tensor_copy(mix[:, KD - 1, t * H:(t + 1) * H], acc[1][:, t, 0:H]).then_inc(out, 1)

            def out_phase(name, post):
                for k in range(KD):
                    split(2 * (UNIT0[name] + k) + 4, 0)
                    if k < KD - 1:
                        out_tile(2 * (UNIT0[name] + k) + 2, k % 2, k)
                    else:
                        last_out(2 * (UNIT0[name] + k) + 2, post)
                    split(2 * (UNIT0[name] + k) + 5, 0)

            def boundary(post, layer, pre_kind=None, pre_layer=None, name=None):
                dve.wait_ge(rstd_ready, 2 * (post + 1))
                pre = (post + 1) // 2
                pg = gain_col(MIX_POST if post % 4 == 1 else FFN_POST, layer)

                def lo(k):
                    if pre < 4 and k >= 0:
                        h_lo_tile(pre, k, gain_col(pre_kind, pre_layer))

                for k in range(KD):
                    if k % 2 == 0:
                        step.mark(dve.tensor_tensor(mix[:, k, :], mix[:, k, :], S[3][:], ALU.mult))
                    else:
                        dve.wait_ge(mix_scaled, KD // 2 * (pre - 1) + 1 + k // 2)
                    lo(k - 2)
                    step.wait(dve)
                    dve.scalar_tensor_tensor(x[:, k, :], mix[:, k, :], col(pg, k), x[:, k, :], ALU.mult, ALU.add
                                             ).then_inc(x_new, 1)
                lo(KD - 2)
                lo(KD - 1)
                if pre < 4:
                    split(2 * UNIT0[name] + 4, 0)

            out_phase("out_ab", 1)
            boundary(1, 0, FFN_PRE, 0, "up0")

            def ffn(layer):
                name = f"up{layer}"

                def first_unit(t):
                    pair = CA + KF * layer
                    if t == 1:
                        dve.wait_ge(sp_ready, pair)
                        dve.wait_ge(sq_added, (KD - 1) * (3 + 4 * layer))
                        first_pair(name, (S[0][:], S[3][:]))
                        dve.wait_ge(rstd_ready, 2 * (3 + 4 * layer))
                        dve.tensor_tensor(S[0][:], S[0][:], rstd[:], ALU.mult).then_inc(rescaled, 1)
                        dve.wait_ge(rescaled, RESCALED[name] + 1)
                    else:
                        split(2 * UNIT0[name] + 7, 0)
                        dve.wait_ge(gate_ready, pair + CA + 1)
                        dve.tensor_tensor(S[3][:], S[3][:], S[2][:], ALU.mult).then_inc(rescaled, 1)
                        dve.wait_ge(g_hi_ready, pair + 1)
                        dve.tensor_tensor(g_lo[:, 0, :], S[3][:], g_hi[:, 0, :], ALU.subtract).then_inc(g_ready, 1)

                def up(i, s_off, first=False):
                    for u in range(2):
                        j = u + 2 * i
                        pair = CA + KF * layer + j
                        w = V_CONVF + layer * 3 * KF
                        for t in range(4):
                            if first and u == 0 and t in (1, 3):
                                first_unit(t)
                                continue
                            for q in halves_at(t, first and u == 0):
                                split(2 * UNIT0[name] + 4 * u + q + s_off, 8 * i if s_off == 0 else 0)
                            if t == 1:
                                dve.wait_ge(half_done, 2 * UNIT0[name] + 4 * u + 2 + 8 * i)
                                dve.wait_ge(sp_ready, pair)
                                dve.tensor_tensor(tok2(S[0][:]), acc_v[0], tok2(rstd[:]), ALU.mult).then_inc(evac, 1)
                            if t == 2:
                                conv(S[0], col(w, j), col(w + KF, j), pair, pair)
                            if t == 3:
                                dve.wait_ge(half_done, 2 * UNIT0[name] + 4 * u + 4 + 8 * i)
                                dve.wait_ge(gate_ready, pair + CA + 1)
                                dve.tensor_tensor(tok2(S[3][:]), acc_v[1], tok2(S[2][:]), ALU.mult).then_inc(evac, 1)
                                dve.wait_ge(g_hi_ready, pair + 1)
                                dve.tensor_tensor(g_lo[:, j, :], S[3][:], g_hi[:, j, :], ALU.subtract
                                                  ).then_inc(g_ready, 1)

                base = step.n
                up(0, 0, True)
                per = step.n - base
                base = step.n
                with dve.Fori(1, KF // 2 - 1) as i:
                    step.n = base + per * (i - 1)
                    up(i, 0)
                step.n = base + per * (KF // 2 - 2)
                up(KF // 2 - 1, 8 * (KF // 2 - 1))
                name = f"down{layer}"

                def down(i, s_off):
                    for e in range(2):
                        for t in range(4):
                            if t == 3 and e == 1 and s_off > 0:
                                last_out(2 * UNIT0[name] + 8 + s_off, 2 + 2 * layer)
                            elif t == 3:
                                out_tile(2 * UNIT0[name] + 4 * e + 4 + 8 * i, e, 2 * i + e)
                            split(2 * UNIT0[name] + 4 * e + t + 4 + s_off, 8 * i if s_off == 0 else 0)

                with dve.Fori(0, KD // 2 - 1) as i:
                    down(i, 0)
                down(KD // 2 - 1, 8 * (KD // 2 - 1))
                if layer == 0:
                    boundary(3, 0, MIX_PRE, 1, "in_c")
                else:
                    boundary(7, 1)

            ffn(0)

            def level_ops(l, cur):
                v = lev[l][:].rearrange("p (n s) -> p n s", s=2 * SPANS[l])
                g = G[:, 0:TP].rearrange("p (n s) -> p n s", s=2 * SPANS[l])
                mid = g[:, :, SPANS[l] - 1:SPANS[l]].broadcast_to([P, TP // (2 * SPANS[l]), 2 * SPANS[l]])
                dve.tensor_tensor(v, g, mid, ALU.subtract).then_inc(C["lev_diff"], 1)

            def level_q(l, cur):
                dve.wait_ge(C["lev_exp"], 4 * cur + l + 1)
                v, q = [z.rearrange("p (n a s) -> p n a s", a=2, s=SPANS[l]) for z in (lev[l][:], qn[:, 0:TP])]
                dve.tensor_tensor(v[:, :, 1, :], v[:, :, 1, :], q[:, :, 1, :], ALU.mult).then_inc(C["lev_ready"], 1)

            def states(prev, cur):
                dve.wait_ge(C["u_done"], cur + 1)
                if prev is not None:
                    dve.wait_ge(state_out, 32 * prev + 32)
                step.mark(dve.tensor_copy(Sst[:, 0, :], A[2][:, 0:P]))
                for c in range(1, NCH):
                    step.wait(dve)
                    i_ = dve.scalar_tensor_tensor(Sst[:, c, :], Sst[:, c - 1, :],
                                                  eG[:, (c + 1) * CH - 1:(c + 1) * CH],
                                                  A[2][:, c * P:(c + 1) * P], ALU.mult, ALU.add)
                    if c < NCH - 1:
                        step.mark(i_)
                i_.then_inc(C["st_ready"], 1)

            def kd_and_level0(cur):
                dve.wait_ge(C["G_ready"], cur + 1)
                gp, gs_ = G[:, 0:TP].rearrange("p (c s) -> p c s", c=NCH), sample(G[:, TP:T])
                dve.tensor_tensor(kd[:, 0:TP].rearrange("p (c s) -> p c s", c=NCH),
                                  gp[:, :, CH - 1:CH].broadcast_to([P, NCH, CH]), gp, ALU.subtract)
                dve.tensor_tensor(sample(kd[:, TP:T]), gs_[:, :, TS - 1:TS].broadcast_to([P, NB, TS]), gs_,
                                  ALU.subtract).then_inc(C["kd_diff"], 1)
                level_ops(0, cur)

            def kdT_lo(cur):
                dve.wait_ge(C["kdT_hi"], cur + 1)
                dve.tensor_tensor(kt_s[R2, :], A[1][R0, 0:P], kt_s[R0, :], ALU.subtract).then_inc(C["kdT_copied"], 1)

            def came(b, which):
                dve.tensor_copy(arrival[0:NB * TS, which:which + 1], A[b][0:NB * TS, 0:1])

            def take_level(prev, which):
                b = (1, 2, 3, 0, 1)[which]
                order = (0, 2, 3, 4, 5)[which]
                dve.wait_ge(C["al_done"], 6 * prev + order + 1)
                if order:
                    dve.wait_ge(C["al_taken"], 6 * prev + order)
                came(b, which)
                if which == 0:
                    at, al = [z[:].rearrange("p (c t) -> p c t", c=NCH) for z in (AT, A[b])]
                    mask = masks[:, 0:1, :].broadcast_to([P, NCH, CH])
                else:
                    span = SPANS[which - 1]
                    n = CH // (2 * span)
                    at = later(AT[:], span).rearrange("p (c n) s -> p c n s", c=NCH)
                    al = A[b][:, 0:TP // 2].rearrange("p (c n s) -> p c n s", c=NCH, s=span)
                    mask = later(masks[:, which, :], span).rearrange("p (c n) s -> p c n s", c=1)
                    mask = mask.broadcast_to([P, NCH, n, span])
                dve.copy_predicated(at, mask, al).then_inc(C["al_taken"], 1)

            def head_out(t, cur):
                u = t // 2
                out = (S[0], qn, vv, gn)[u]
                if isinstance(cur, int) and cur == 0 and t == 1:
                    dve.wait_ge(sq_added, (KD - 1) * 5)
                    first_pair("in_c", (S[0][:], qn[:]))
                    dve.wait_ge(rstd_ready, 10)
                    dve.tensor_tensor(S[0][:], S[0][:], rstd[:], ALU.mult).then_inc(rescaled, 1)
                    dve.wait_ge(rescaled, RESCALED["in_c"] + 1)
                else:
                    dve.wait_ge(half_done, 2 * UNIT0["in_c"] + t + 1 + 8 * cur)
                    dve.tensor_tensor(tok2(out[:]), acc_v[u % 2], tok2(rstd[:]), ALU.mult).then_inc(evac, 1)
                if t == 1:
                    dve.wait_ge(evac, tile("in_c", 0) + 4 * cur)
                    dve.tensor_scalar(S[0][:], S[0][:], -80.0, None, ALU.max).then_inc(C["fl_ready"], 1)
                    if isinstance(cur, int) and cur == 0:
                        dve.tensor_tensor(qn[:], qn[:], rstd[:], ALU.mult).then_inc(rescaled, 1)
                        dve.wait_ge(rescaled, RESCALED["in_c"] + 2)
                if t == 7:
                    dve.wait_ge(evac, tile("in_c", 3) + 4 * cur)
                    dve.tensor_scalar(sg[:], gn[:], -80.0, None, ALU.max).then_inc(C["gn_ready"], 1)

            def hgrn_tick(t, prev, cur):
                if prev is not None:
                    if t == 0:
                        take_level(prev, 0)
                        dve.wait_ge(C["al_done"], 6 * prev + 2)
                        came(2, 5)
                        dve.copy_predicated(AT_s[:], mask_s[:], A[2][0:NB * TS, 0:NB * TS]).then_inc(C["al_taken"], 1)
                    if t == 1:
                        take_level(prev, 1)
                        take_level(prev, 2)
                    if t == 2:
                        take_level(prev, 3)
                        take_level(prev, 4)
                        dve.wait_ge(C["v_lo"], prev + 1)
                        v3 = v3_s[:].rearrange("p (a b) -> p a b", a=1).broadcast_to([3 * NB * TS, NB, P])
                        dve.tensor_tensor(vbd[:], v3, own[:], ALU.mult).then_inc(C["vbd_ready"], 1)
                    if t == 4:
                        dve.wait_ge(C["osq_ready"], prev + 1)
                        dve.wait_ge(C["gs_ready"], prev + 1)
                        dve.scalar_tensor_tensor(sg[:, 0:TP], A[3][:], vec[:, V_NG:V_NG + 1], sg[:, 0:TP],
                                                 ALU.mult, ALU.mult)
                        dve.scalar_tensor_tensor(sg[:, TP:T], A[2][:, 0:NB * TS], vec[:, V_NG:V_NG + 1],
                                                 sg[:, TP:T], ALU.mult, ALU.mult).then_inc(C["og_ready"], 1)
                    if t == 5:
                        dve.wait_ge(C["ors_ready"], prev + 1)
                        dve.wait_ge(C["og_ready"], prev + 1)
                        dve.tensor_tensor(S[3][:], S[3][:], sg[:], ALU.mult).then_inc(C["oy_ready"], 1)
                        if cur is not None:
                            level_ops(2, cur)
                            kdT_lo(cur)
                        dve.wait_ge(C["oy_hi"], prev + 1)
                        dve.tensor_tensor(y_lo[:, prev, :], S[3][:], y_hi[:, prev, :], ALU.subtract
                                          ).then_inc(C["oy_lo"], 1)
                if prev is not None and t == 3:
                    if cur is not None:
                        kd_and_level0(cur)
                    dve.wait_ge(C["s0_scaled"], prev + 1)
                    for z in range(2):
                        dve.wait_ge(C["us_done"], 2 * prev + 1 + z)
                        half_b = slice(4 * z, 4 * z + 4)
                        dve.tensor_tensor(Snew[:, half_b, :], Snew[:, half_b, :],
                                          A[z][:].rearrange("p (a b) -> p a b", a=4), ALU.add).then_inc(C["snew_ready"], 1)
                if cur is None:
                    return
                if t == 2:
                    dve.wait_ge(C["sig_ready"], cur + 1)
                    one_lb = lb[:, 7, cur:cur + 1] if isinstance(cur, int) else lb[:, 7, bass.ds(cur, 1)]
                    low = lb[:, 6, cur:cur + 1] if isinstance(cur, int) else lb[:, 6, bass.ds(cur, 1)]
                    dve.scalar_tensor_tensor(kk[:], S[0][:], one_lb, S[1][:], ALU.mult, ALU.mult)
                    step.mark(dve.tensor_scalar(S[1][:], S[1][:], one_lb, low, ALU.mult, ALU.add))
                    step.wait(dve)
                    dve.tensor_scalar(S[1][:], S[1][:], F_FLOOR, None, ALU.max).then_inc(C["ff_ready"], 1)
                    dve.wait_ge(C["lf_ready"], cur + 1)
                    dve.tensor_tensor_scan(G[:], keep[:], S[1][:], 0.0, ALU.mult, ALU.add).then_inc(C["G_ready"], 1)
                if prev is None and t == 3:
                    kd_and_level0(cur)
                if t == 4:
                    level_ops(1, cur)
                    level_q(0, cur)
                if t == 5:
                    if prev is None:
                        level_ops(2, cur)
                    if prev is None:
                        kdT_lo(cur)
                    gp, gs_ = G[:, 0:TP].rearrange("p (c s) -> p c s", s=8), sample(G[:, TP:T])
                    dve.tensor_tensor(E2[:, 0:TP].rearrange("p (c s) -> p c s", s=8), gp,
                                      gp[:, :, 3:4].broadcast_to([P, TP // 8, 8]), ALU.subtract)
                    dve.tensor_tensor(sample(E2[:, TP:T]), gs_, gs_[:, :, 1:2].broadcast_to([P, NB, TS]),
                                      ALU.subtract).then_inc(C["diag_diff"], 1)
                    level_q(1, cur)
                if t == 6:
                    level_ops(3, cur)
                    level_q(2, cur)
                    dve.wait_ge(C["v_hi"], cur + 1)
                    dve.tensor_tensor(v3_s[R1, :], vt_s[:], v_hi_s[:], ALU.subtract).then_inc(C["v_lo"], 1)
                    dve.wait_ge(C["diag_exp"], cur + 1)
                    dve.tensor_tensor(E2[:], E2[:], kk[:], ALU.mult).then_inc(C["diag_ready"], 1)
                if t == 7:
                    level_q(3, cur)

            def head(hd, prev, s_off):
                for t in range(8):
                    first = prev is None and t < 4
                    if t % 2 and not (first and t == 3):
                        head_out(t, hd)
                    if t == 7:
                        states(prev, hd)
                    for q in halves_at(t, prev is None):
                        if not (first and t == 1):
                            split(2 * UNIT0["in_c"] + q + s_off, 8 * hd if s_off == 0 else 0)
                    hgrn_tick(t, prev, hd)

            lower_bounds_b()
            step.wait(dve)
            dve.wait_ge(const_c, 64)
            dve.wait_ge(set_up, 5)
            head(0, None, 0)
            base, STEPS_C = step.n, 4
            with dve.Fori(1, HEADS - 1) as hd:
                step.n = base + STEPS_C * (hd - 1)
                head(hd, hd - 1, 0)
            step.n = base + STEPS_C * (HEADS - 2)
            head(HEADS - 1, HEADS - 2, 8 * (HEADS - 1))
            assert step.n == base + STEPS_C * (HEADS - 1), step.n - base
            for t in range(6):
                hgrn_tick(t, HEADS - 1, None)
            out_phase("out_c", 3)
            boundary(5, 1, FFN_PRE, 1, "up1")
            ffn(1)

        @block.gpsimd
        def _(pool):
            pool.memset(ones[:], 1.0).then_inc(set_up, 1)
            pool.memset(eps[:], EPS).then_inc(set_up, 1)
            pool.memset(qbd[:], 0.0).then_inc(set_up, 1)
            step = Steps(pool_step)

            def add_squares(norm, post=False):
                def scale(i):
                    k = 2 * i + 1
                    pool.tensor_tensor(mix[:, k, :], mix[:, k, :], S[3][:], ALU.mult).then_inc(mix_scaled, 1)

                def add(k):
                    pool.wait_ge(sq_ready, KD * norm + 1 + k)
                    pool.wait_ge(sq_added, (KD - 1) * norm + k)
                    e = k % 2 if isinstance(k, int) else 0
                    pool.tensor_tensor(S[2][:], S[2][:], S[e][:], ALU.add).then_inc(sq_added, 1)

                if post:
                    pool.wait_ge(rstd_ready, 2 * norm)
                    scale(0)
                    scale(1)
                if norm < 8:
                    if norm:
                        pool.wait_ge(stat_done, 2 * norm)
                    pool.wait_ge(sq_ready, KD * norm + 2)
                    pool.tensor_tensor(S[2][:], S[0][:], S[1][:], ALU.add).then_inc(sq_added, 2)
                if post:
                    scale(2)
                if norm < 8:
                    add(2)
                    add(3)
                if post:
                    scale(3)
                if norm < 8:
                    add(4)
                    add(5)
                    add(6)

            def conv_side(src, state, tail, count, input_out, ready=evac):
                pool.wait_ge(ready, input_out)
                if not isinstance(count, int) or count:
                    pool.wait_ge(conv_done, count)
                step.mark(pool.tensor_copy(sp[:, :, 0:2], state()))
                step.mark(pool.tensor_copy(sp[:, :, 2:2 + TS], sample(src[:, TP:T])))
                step.wait(pool)
                step.mark(pool.tensor_copy(tail(), src[:, TP - 2:TP]))
                pool.tensor_copy(state(), sp[:, :, TS:TS + 2]).then_inc(sp_ready, 1)

            add_squares(0)
            pool.wait_ge(const_in, 48)
            pool.wait_ge(evac, tile("in_ab", 3))
            pool.wait_ge(rescaled, 2)
            pool.wait_ge(set_up, 3)
            for g in range(2):
                r = slice(64 * g, 64 * g + 64)
                if g:
                    pool.wait_ge(qbd_ready, 1)
                pool.tensor_copy(qbd[r, :, 16 * g:16 * g + 16].rearrange("p b (j t) -> p j b t", j=GRP),
                                 q_sb[r, :, TP:T].rearrange("p j (b t) -> p j b t", b=NB)).then_inc(qbd_ready, 1)
            pool.wait_ge(evac, tile("in_ab", 4))
            pool.wait_ge(qbd_ready, 2)
            pool.tensor_copy(kc[:, :, WIN:WIN + TS], sample(k_sb[:, TP:T])).then_inc(kc_ready, 1)

            def normalise(s):
                pool.wait_ge(p_sum, 2 * s + 4)
                if s < 0:
                    z = sm_s[:, 5, :].rearrange("p (c a) -> p c a", a=1).broadcast_to([P, 2, WIN + TS])
                    pool.tensor_tensor(pr_s[:], pr_s[:], z, ALU.mult).then_inc(p_ready, 1)
                    return
                w = slice(WIN, 2 * WIN) if s < 2 else slice(0, 2 * WIN)
                p = pr[s % 2][:, :, w]
                z = sm[:, s % 2, 5, :].rearrange("p (c a) -> p c a", a=1).broadcast_to([P, GRP, 128 if s < 2 else 256])
                pool.tensor_tensor(p, p, z, ALU.mult).then_inc(p_ready, 1)

            steps_of = {13: [-1]}
            for s in range(8):
                steps_of.setdefault(15 + 2 * s, []).append(s)
            for m in range(12, 36):
                c, r = divmod(m - 12, 6)
                if r == 1:
                    pool.wait_ge(evac, tile("in_ab", 6 + 3 * c))
                    pool.tensor_tensor(S[0][:], S[0][:], rstd[:], ALU.mult).then_inc(gate_ready, 1)
                if r == 3:
                    conv_side(S[3], lambda: st_a[:, c, :, :], lambda: tail_a[:, c, :], c, tile("in_ab", 7 + 3 * c))
                if r == 4:
                    pool.wait_ge(conv_done, c + 1)
                    pool.tensor_tensor(S[1][:], S[1][:], rstd[:], ALU.mult).then_inc(gate_ready, 1)
                for s in steps_of.get(m, []):
                    normalise(s)
            add_squares(1)
            add_squares(2, post=True)

            def ffn(layer):
                base = step.n

                def gate(j, ready, count):
                    pair = CA + KF * layer + j
                    conv_side(S[0], lambda: st_f[:, layer, j, :, :], lambda: tail_f[:, layer, j, :], pair, count, ready)
                    pool.wait_ge(act_done, KF * layer + j + 1)
                    pool.tensor_tensor(S[2][:], S[2][:], rstd[:], ALU.mult).then_inc(gate_ready, 1)

                gate(0, rescaled, RESCALED[f"up{layer}"] + 1)
                with pool.Fori(1, KF) as j:
                    step.n = base + 3 * j
                    gate(j, evac, tile(f"up{layer}", 0) + 2 * j)
                step.n = base + 3 * KF
                if layer == 1:
                    pool.wait_ge(sp_ready, CA + 2 * KF)
                    step.wait(pool)
                    for out, state in (("o_ca", tail_a), ("o_cs", st_a), ("o_fp", tail_f), ("o_fs", st_f)):
                        pool.dma_start(dram[out], state[:]).then_inc(conv_states_out, 16)
                pool.wait_ge(evac, tile(f"up{layer}", 2 * KF - 1))
                add_squares(3 + 4 * layer)
                add_squares(4 + 4 * layer, post=True)

            ffn(0)

            def hgrn(prev, cur):
                if prev is not None:
                    pool.wait_ge(C["sg_ready"], prev + 1)
                    pool.tensor_tensor(sg[:], sg[:], gn[:], ALU.mult).then_inc(C["gs_ready"], 1)
                if cur is not None:
                    pool.wait_ge(C["kd_exp"], cur + 1)
                    pool.tensor_tensor(kd[:], kd[:], kk[:], ALU.mult).then_inc(C["kd_ready"], 1)
                if cur is not None:
                    for l in range(3):
                        key_level(l, cur)
                        if l == 0:
                            if prev is not None:
                                pool.wait_ge(C["oc_done"], prev + 1)
                            pool.wait_ge(C["eG_ready"], cur + 1)
                            if prev is None:
                                pool.wait_ge(rescaled, RESCALED["in_c"] + 2)
                            pool.wait_ge(evac, tile("in_c", 1) + 4 * cur)
                            pool.tensor_tensor(qG[:], eG[:], qn[:], ALU.mult).then_inc(C["qG_ready"], 1)
                    pool.wait_ge(C["diag_exp"], cur + 1)
                    pool.tensor_tensor(E1[:], E1[:], qn[:], ALU.mult).then_inc(C["diag_ready"], 1)
                    pool.wait_ge(state0_in, 16 * cur + 16)
                    if prev is not None:
                        pool.wait_ge(state_out, 32 * prev + 32)
                    e = sample(eG[:, TP:T])[:, :, TS - 1:TS].broadcast_to([P, NB, P])
                    pool.tensor_tensor(Snew[:], S0[:], e, ALU.mult).then_inc(C["s0_scaled"], 1)
                    key_level(3, cur)

            def key_level(l, cur):
                pool.wait_ge(C["lev_exp"], 4 * cur + l + 1)
                v, k_ = [z.rearrange("p (n a s) -> p n a s", a=2, s=SPANS[l]) for z in (lev[l][:], kk[:, 0:TP])]
                pool.tensor_tensor(v[:, :, 0, :], v[:, :, 0, :], k_[:, :, 0, :], ALU.mult).then_inc(C["lev_ready"], 1)

            pool.wait_ge(half_done, 2 * UNIT0["in_c"])
            pool.memset(AT[:], 0.0).then_inc(set_up, 1)
            pool.memset(AT_s[:], 0.0).then_inc(set_up, 1)
            hgrn(None, 0)
            with pool.Fori(1, HEADS) as hd:
                hgrn(hd - 1, hd)
            hgrn(HEADS - 1, None)
            pool.wait_ge(C["osq_ready"], HEADS)
            pool.wait_ge(C["ostat_done"], HEADS)
            add_squares(5)
            add_squares(6, post=True)
            ffn(1)

            pool.wait_ge(stored, 16 * 5)
            pool.wait_ge(conv_states_out, 16 * 4)
            pool.wait_ge(state_out, 32 * HEADS)


def _layouts(a):
    f = {k: np.asarray(v) for k, v in a.items()}
    xt = np.concatenate([f["x_prompt"][0], f["x_sample"].reshape(NB * TS, D)], 0).T

    def units(w, cols, kt=8):
        out = []
        for r0, c in cols:
            blk = w[r0:r0 + kt * P, c] if isinstance(c, np.ndarray) else w[r0:r0 + kt * P, c:c + P]
            out.append(blk.reshape(kt, P, P).transpose(1, 0, 2).reshape(P, kt * P))
        return np.stack(out)

    h0 = np.arange(HD)
    pair = [np.concatenate([j * HD + h0, (GRP + j) * HD + h0]) for j in range(GRP)]
    q0 = 3 * A_W
    ab = [(0, q0 + pair[j]) for j in range(GRP)] + [(0, q0 + 512), (0, q0 + 640)]
    for c in range(CA):
        ab += [(0, c * P), (0, 2 * A_W + c * P), (0, A_W + c * P)]
    rows = np.concatenate([A_W + p for p in pair] + [np.arange(A_W)])
    d = {"xT": xt.reshape(KD, P, T).transpose(1, 0, 2),
         "w_in_ab": units(f["w_in_ab"][0], ab),
         "w_out_ab": units(f["w_out_ab"][0][rows], [(0, k * P) for k in range(KD)]),
         "w_in_c": units(f["w_in_c"][0], [(0, o + h * P) for h in range(HEADS) for o in (D, 0, 2 * D, 3 * D)]),
         "w_out_c": units(f["w_out_c"][0], [(0, k * P) for k in range(KD)])}
    for l in range(2):
        d[f"w_up{l}"] = units(f["w_ffn_up"][l], [(0, o + j * P) for j in range(KF) for o in (0, DFF)])
        d[f"w_down{l}"] = units(f["w_ffn_down"][l], [(r * KFH * P, k * P) for k in range(KD) for r in range(2)], KFH)

    def cols(v):
        return v.reshape(-1, P).T

    sinks = f["attn_sinks"][0]
    row = np.arange(P)
    d["vec"] = np.concatenate(
        [cols(f[n][l]) for n in ("norm_mix_pre", "norm_mix_post", "norm_ffn_pre", "norm_ffn_post") for l in range(2)]
        + [cols(f["conv_a_w"][0][t]) for t in range(3)] + [cols(f["ffn_conv_w"][l][t]) for l in range(2) for t in range(3)]
        + [cols(f["hgrn_lb_logits"][l]) for l in range(2)] + [cols(f["hgrn_norm_g"][0])]
        + [np.broadcast_to(sinks, (P, 8)), sinks[4 * (row // 16 % 2) + row // 4 % 4][:, None]], 1)
    d["st_a"] = f["state_conv_a"][0].reshape(NB, 2, CA, P).transpose(3, 2, 0, 1)
    d["st_f"] = f["state_ffn_conv"].reshape(2, NB, 2, KF, P).transpose(4, 0, 3, 1, 2)
    d["kcT"] = f["cache_swa_k"][0].reshape(NB, WIN, P).transpose(2, 0, 1)
    d["vc"] = f["cache_swa_v"][0].reshape(NB, WIN, P)
    d["state0"] = f["state_hgrn"][0].transpose(1, 2, 0, 3)
    return d


_OUTS = {"o_x": (P, KD, T), "o_kp": (P, WIN), "o_ks": (P, NB, WIN), "o_vp": (WIN, P), "o_vs": (NB, WIN, P),
         "o_ca": (P, CA, 2), "o_cs": (P, CA, NB, 2), "o_fp": (P, 2, KF, 2), "o_fs": (P, 2, KF, NB, 2),
         "o_sp": (HEADS, P, P), "o_ss": (HEADS, P, NB, P)}


def kernel(**inputs):
    import concourse.bacc as bacc
    from concourse.bass_utils import run_bass_kernel_spmd

    nc = bacc.Bacc("TRN2", target_bir_lowering=False, num_devices=1)
    arrays, dram = {}, {}
    for name, a in {**_layouts(inputs), **shape_tables()}.items():
        a = np.ascontiguousarray(a)
        arrays["in_" + name] = a
        dram[name] = nc.dram_tensor("in_" + name, a.shape, mybir.dt.from_np(a.dtype), kind="ExternalInput").ap()
    for name, shape in _OUTS.items():
        dram[name] = nc.dram_tensor(name, shape, F32, kind="ExternalOutput").ap()
    build(nc, dram)
    o = run_bass_kernel_spmd(nc, [arrays], core_ids=[0]).results[0]
    o = {n: np.asarray(o[n]).reshape(s) for n, s in _OUTS.items()}

    y = o["o_x"].transpose(2, 1, 0).reshape(T, D)
    kv = (1, WIN, 2, HD)
    return (y[:TP].reshape(1, TP, D), y[TP:].reshape(NB, TS, D),
            o["o_ca"].transpose(2, 1, 0).reshape(1, 1, 2, A_W),
            o["o_cs"].transpose(2, 3, 1, 0).reshape(1, NB, 2, A_W),
            o["o_kp"].T.reshape(1, *kv), o["o_ks"].transpose(1, 2, 0).reshape(1, NB, *kv[1:]),
            o["o_vp"].reshape(1, *kv), o["o_vs"].reshape(1, NB, *kv[1:]),
            o["o_sp"].reshape(1, 1, HEADS, P, P), o["o_ss"].transpose(2, 0, 1, 3).reshape(1, NB, HEADS, P, P),
            o["o_fp"].transpose(1, 3, 2, 0).reshape(2, 1, 2, DFF),
            o["o_fs"].transpose(1, 3, 4, 2, 0).reshape(2, NB, 2, DFF))
```
